# Optimizing a Trainium2 kernel written in Bass

```python
import math
import jax, jax.numpy as jnp
from jax import lax
import numpy as np

D_MODEL = 1024
BATCH = 1
SEQ = 512
DEPTH = 1

POOL_WINDOWS = (2, 4, 8, 16)
POOL_WIDTH = D_MODEL // 2
POOL_GROUP = POOL_WIDTH // len(POOL_WINDOWS)
ATTN_WIDTH = D_MODEL - POOL_WIDTH
HEAD_DIM = 64
N_HEADS = ATTN_WIDTH // HEAD_DIM
IN_WIDTH = POOL_WIDTH + 3 * ATTN_WIDTH
MOBA_BLOCK = 256
MOBA_TOP_K = 3
QUERY_CHUNK = 32
NUM_BUCKETS = 32
MAX_DISTANCE = 128
D_FF = 4 * D_MODEL
EPS = 1e-6

kernel_name = "hymba_pool_moba_sandwich_block"

def rmsnorm(x, g):
    xf = x.astype(jnp.float32)
    y = xf * lax.rsqrt(jnp.mean(xf * xf, axis=-1, keepdims=True) + EPS)
    return (y * g.astype(jnp.float32)).astype(x.dtype)

def t5_bucket(dist):
    n = jnp.maximum(dist, 0)
    max_exact = NUM_BUCKETS // 2
    n_safe = jnp.maximum(n, max_exact).astype(jnp.float32)
    large = max_exact + (jnp.log(n_safe / max_exact) / math.log(MAX_DISTANCE / max_exact)
                         * (NUM_BUCKETS - max_exact)).astype(jnp.int32)
    large = jnp.minimum(large, NUM_BUCKETS - 1)
    return jnp.where(n < max_exact, n, large)

def pool_mixer(u, w_pool, pool_scale):
    b, s, _ = u.shape
    uf = u.astype(jnp.float32).reshape(b, s, len(POOL_WINDOWS), POOL_GROUP)
    csum = jnp.cumsum(uf, axis=1)
    pos = jnp.arange(1, s + 1, dtype=jnp.float32)
    pooled = []
    for gi, w in enumerate(POOL_WINDOWS):
        c = csum[:, :, gi]
        prev = jnp.pad(c, ((0, 0), (w, 0), (0, 0)))[:, :s]
        cnt = jnp.minimum(pos, float(w))[None, :, None]
        pooled.append((c - prev) / cnt)
    mixed = (jnp.stack(pooled, axis=2) - uf).astype(u.dtype)
    y = jnp.einsum('bsgc,gcd->bsgd', mixed, w_pool).reshape(b, s, POOL_WIDTH)
    return y * pool_scale

def moba_attention(q, k, v, rel_bias):
    b, s, h, dh = q.shape
    n_blocks = -(-s // MOBA_BLOCK)
    s_pad = n_blocks * MOBA_BLOCK
    pad = ((0, 0), (0, s_pad - s), (0, 0), (0, 0))
    q, k, v = [jnp.pad(t, pad).transpose(0, 2, 1, 3) for t in (q, k, v)]
    scale = HEAD_DIM ** -0.5
    k_blocks = k.reshape(b, h, n_blocks, MOBA_BLOCK, dh)
    v_blocks = v.reshape(b, h, n_blocks, MOBA_BLOCK, dh)

    k_mean = jnp.mean(k_blocks.astype(jnp.float32), axis=3)
    gate = jnp.einsum('bhsd,bhnd->bhsn', q.astype(jnp.float32), k_mean)
    q_block = jnp.arange(s_pad) // MOBA_BLOCK
    past = jnp.arange(n_blocks)[None, :] < q_block[:, None]
    gate = jnp.where(past, gate, -jnp.inf)
    top_k = min(MOBA_TOP_K, n_blocks)
    _, sel = lax.top_k(gate, top_k)
    sel_valid = sel < q_block[:, None]

    n_chunks = s_pad // QUERY_CHUNK

    def to_chunks(t):
        t = t.reshape((b, h, n_chunks, QUERY_CHUNK) + t.shape[3:])
        return jnp.moveaxis(t, 2, 0)

    bias_table = rel_bias.T.astype(jnp.float32)
    bi = jnp.arange(b)[:, None, None, None]
    hi = jnp.arange(h)[None, :, None, None]
    offs = jnp.arange(MOBA_BLOCK)

    def chunk_attn(args):
        q_c, sel_c, valid_c, ci = args
        q_pos = ci * QUERY_CHUNK + jnp.arange(QUERY_CHUNK)
        k_sel = k_blocks[bi, hi, sel_c]
        v_sel = v_blocks[bi, hi, sel_c]
        s_sel = jnp.einsum('bhcd,bhcknd->bhckn', q_c, k_sel).astype(jnp.float32) * scale
        k_pos_sel = sel_c[..., None] * MOBA_BLOCK + offs
        s_sel = s_sel + bias_table[hi[..., None], t5_bucket(q_pos[:, None, None] - k_pos_sel)]
        s_sel = jnp.where(valid_c[..., None], s_sel, -jnp.inf)
        s_sel = s_sel.reshape(b, h, QUERY_CHUNK, top_k * MOBA_BLOCK)
        own = (ci * QUERY_CHUNK) // MOBA_BLOCK
        k_own = lax.dynamic_index_in_dim(k_blocks, own, axis=2, keepdims=False)
        v_own = lax.dynamic_index_in_dim(v_blocks, own, axis=2, keepdims=False)
        dist_own = q_pos[:, None] - (own * MOBA_BLOCK + offs)[None, :]
        s_own = (jnp.einsum('bhcd,bhnd->bhcn', q_c, k_own).astype(jnp.float32) * scale
                 + bias_table[:, t5_bucket(dist_own)][None])
        s_own = jnp.where(dist_own >= 0, s_own, -jnp.inf)
        p = jax.nn.softmax(jnp.concatenate([s_sel, s_own], axis=-1), axis=-1).astype(v.dtype)
        p_sel = p[..., :top_k * MOBA_BLOCK].reshape(b, h, QUERY_CHUNK, top_k, MOBA_BLOCK)
        p_own = p[..., top_k * MOBA_BLOCK:]
        return (jnp.einsum('bhckn,bhcknd->bhcd', p_sel, v_sel)
                + jnp.einsum('bhcn,bhnd->bhcd', p_own, v_own))

    out = lax.map(chunk_attn, (to_chunks(q), to_chunks(sel), to_chunks(sel_valid),
                               jnp.arange(n_chunks, dtype=jnp.int32)))
    out = jnp.moveaxis(out, 0, 2).reshape(b, h, s_pad, dh)[:, :, :s]
    return out.transpose(0, 2, 1, 3).reshape(b, s, h * dh)

def setup_inputs(seed: int = 0) -> dict:
    key = jax.random.key(seed)
    ks = jax.random.split(key, 16)
    L = DEPTH
    nrm = lambda k, shape, sc: jax.random.normal(k, shape, jnp.float32) * sc
    gain = lambda k, shape: 1.0 + 0.05 * jax.random.normal(k, shape, jnp.float32)
    return {
        "x": jax.random.normal(ks[0], (BATCH, SEQ, D_MODEL), jnp.float32),
        "g_mix_pre": gain(ks[1], (L, D_MODEL)),
        "w_in": nrm(ks[2], (L, D_MODEL, IN_WIDTH), D_MODEL ** -0.5),
        "w_pool": nrm(ks[3], (L, len(POOL_WINDOWS), POOL_GROUP, POOL_GROUP), POOL_GROUP ** -0.5),
        "pool_scale": 1.0 + 0.1 * jax.random.normal(ks[4], (L, POOL_WIDTH), jnp.float32),
        "rel_bias": nrm(ks[5], (NUM_BUCKETS, N_HEADS), 0.5),
        "g_pool_out": gain(ks[6], (L, POOL_WIDTH)),
        "g_attn_out": gain(ks[7], (L, ATTN_WIDTH)),
        "w_out": nrm(ks[8], (L, D_MODEL, D_MODEL), D_MODEL ** -0.5),
        "g_mix_post": gain(ks[9], (L, D_MODEL)),
        "g_mlp_pre": gain(ks[10], (L, D_MODEL)),
        "w_up": nrm(ks[11], (L, D_MODEL, D_FF), D_MODEL ** -0.5),
        "w_down": nrm(ks[12], (L, D_FF, D_MODEL), D_FF ** -0.5),
        "g_mlp_post": gain(ks[13], (L, D_MODEL)),
    }

def reference(x, g_mix_pre, w_in, w_pool, pool_scale, rel_bias, g_pool_out, g_attn_out,
              w_out, g_mix_post, g_mlp_pre, w_up, w_down, g_mlp_post):
    b, s, _ = x.shape
    for i in range(DEPTH):
        h = rmsnorm(x, g_mix_pre[i])
        z = h @ w_in[i]
        u, q, k, v = jnp.split(z, [POOL_WIDTH, POOL_WIDTH + ATTN_WIDTH,
                                   POOL_WIDTH + 2 * ATTN_WIDTH], axis=-1)
        y_pool = rmsnorm(pool_mixer(u, w_pool[i], pool_scale[i]), g_pool_out[i])
        y_attn = moba_attention(q.reshape(b, s, N_HEADS, HEAD_DIM),
                                k.reshape(b, s, N_HEADS, HEAD_DIM),
                                v.reshape(b, s, N_HEADS, HEAD_DIM), rel_bias)
        y_attn = rmsnorm(y_attn, g_attn_out[i])
        mix = jnp.concatenate([y_pool, y_attn], axis=-1) @ w_out[i]
        x = x + rmsnorm(mix, g_mix_post[i])
        h = rmsnorm(x, g_mlp_pre[i])
        ff = jnp.square(jax.nn.relu(h @ w_up[i])) @ w_down[i]
        x = x + rmsnorm(ff, g_mlp_post[i])
    return x


_drawn_inputs = setup_inputs


def setup_inputs(seed=0):
    import zlib

    import numpy as np

    out = dict(_drawn_inputs(seed))
    spreads = {}
    factors = {}
    for name, (base, spread) in spreads.items():
        noise = np.random.default_rng([zlib.crc32(name.encode()), seed]).standard_normal(out[name].shape)
        drawn = base * np.exp(spread * noise) if base else spread * noise
        out[name] = __import__('jax').numpy.asarray(drawn.astype(out[name].dtype))
    for name, factor in factors.items():
        out[name] = (out[name] * factor).astype(out[name].dtype)
    return out
```

```python
from contextlib import ExitStack

import concourse.bass as bass
from concourse import mybir

F32 = mybir.dt.float32
F16 = mybir.dt.float16
ALU = mybir.AluOpType
ACT = mybir.ActivationFunctionType
AX = mybir.AxisListType.X
ds = bass.ds

P = 128
SEQ, D = 512, 1024
NT = SEQ // P
KC = D // P
HALF = 512
POOL_W = D // 2
WINDOWS = (2, 4, 8, 16)
NG = len(WINDOWS)
PAD = max(WINDOWS)
HD = 64
NPAIR = POOL_W // P
STEPS = 2 * NT
D_FF = 4 * D
NF = D_FF // P
BUCKETS = 32
NEAR = 2 * P
SPAN = 3 * P
WS = 32.0
EPS = 1e-6
MASKED = -1e30
UNIT = 1024
RAW = 4

SLOT_V = 0
SLOT_Q, SLOT_K, SLOT_U = 4, 5, 6
U_ORDER = (3, 0, 1, 2)
SLOT_YA, SLOT_YP = 0, 4
SLOT_SQ = 2
SLOT_MIX = (7, 8, 10, 11)
D_WO, D_UP = 8, 12
ND = NF // 2


def loads_until(d):
    return sum(32 if 2 <= e < D_WO else 16 for e in range(d % RAW, d + 1, RAW))


def hybrid_layer(nc, x, w_in, w_pool, pool_scale, rel_bias, g_mix_pre, g_pool_out, g_attn_out,
                 w_out, g_mix_post, g_mlp_pre, w_up, w_down, g_mlp_post, bucket_rows, edge_ratio, out):
    ctx = ExitStack()
    with ctx:
        def sb(name, shape, dt=F32):
            return ctx.enter_context(nc.sbuf_tensor(name, shape, dt))

        def sem(name):
            return ctx.enter_context(nc.semaphore(name))

        x_tok = sb("x_tok", [P, NT, D])
        hT = sb("hT", [P, 2, KC, SEQ], F16)
        raw = sb("raw", [P, RAW, 2 * UNIT])
        big = sb("big", [P, 16, 2, UNIT], F16)
        wo = sb("wo", [P, KC, 2, UNIT], F16)
        ring = sb("ring", [P, 4, 2, UNIT], F16)
        scr = sb("scr", [P, 6144])
        ident = sb("ident", [P, P])
        reverse = sb("reverse", [P, P])
        ones = sb("ones", [P, 1])
        nhalf = sb("nhalf", [P, NT])
        ratio = sb("ratio", [P, NG, PAD])
        wp = sb("wp", [P, 2, NG, P], F16)
        vecs = sb("vecs", [P, 5 * NG])
        zero16 = sb("zero16", [P, P], F16)
        stat = sb("stat", [P, 112])

        flat = big[:, :, :, :].rearrange("p s a n -> p (s a n)")
        aT = flat.rearrange("p (j a n) -> p j a n", j=NF, a=2)
        v_hi = ring[:, 0, :, :].rearrange("p a (t n) -> p (a t) n", n=HALF)
        v_lo = ring[:, 1, :, :].rearrange("p a (t n) -> p (a t) n", n=HALF)
        bias = ring[:, 2:4, :, :].rearrange("p s a n -> p (s a n)").bitcast(F32)
        late = big[:, 14:16, :, :].rearrange("p s a n -> p (s a n)").bitcast(F32)
        onehot, diag_row, wp_raw = late[0:BUCKETS + 1, 0:SPAN], late[0:8, 384:384 + SPAN], late[:, 1024:1536]
        windows = wo[:, 0:2, :, :].rearrange("p s a n -> p (s a n)").bitcast(F32)
        vec_rows, rel_tab = late[0:3 * NG, 768:896], late[0:BUCKETS + 1, 896:904]

        def mix(t):
            return big[:, SLOT_MIX[t], :, :].rearrange("p a n -> p (a n)").bitcast(F32)

        def y_half(slot, c):
            return big[:, slot + c // 2, c % 2, :].rearrange("p (a n) -> p a n", a=2)

        sq_pool = big[:, SLOT_SQ:SLOT_SQ + 2, :, :].rearrange("p s a n -> p (s a n)").bitcast(F32)
        mixed = [big[:, SLOT_U + 3 * n, 0, :].rearrange("p (a n) -> p a n", a=2) for n in range(NG)]

        xs = [scr[:, UNIT * t:UNIT * (t + 1)] for t in range(NT)]
        row_pre, junk0 = scr[:, 4096:5120], scr[:, 5120:6144]
        prob = [scr[:, 0:512], scr[:, 512:1024]]
        pT = [scr[:, 1024 + 512 * b:1536 + 512 * b].bitcast(F16).rearrange("p (a n) -> p a n", a=2) for b in range(2)]
        qT = scr[:, 2048:2560].bitcast(F16).rearrange("p (a n) -> p a n", a=2)
        kT = scr[:, 2560:3072].bitcast(F16).rearrange("p (a n) -> p a n", a=2)
        u_pad, win_a, win_b = (scr[:, 3072 + 528 * n:3600 + 528 * n] for n in range(3))
        y_tok = scr[:, 4656:5168].rearrange("p (t n) -> p t n", t=NT)
        junk1 = scr[:, 5168:5680]
        xs2 = [scr[:, 0:1024], scr[:, 1024:2048]]
        row_mix_post, row_mlp_pre, junk2, row_mlp_post = (scr[:, 2048 + 1024 * n:3072 + 1024 * n] for n in range(4))
        relu = [scr[:, 0:512], scr[:, 512:1024]]
        squared = [scr[:, 1024:1536], scr[:, 1536:2048]]
        y_out = [scr[:, 0:1024], scr[:, 1024:2048]]

        ss_x, r_x = stat[:, 0:4], stat[:, 4:8]
        neg_max, row_sum, row_inv = stat[:, 8:12], stat[:, 12:16], stat[:, 16:20]
        ss_attn = stat[:, 20:36]
        r_pool, r_attn = stat[:, 36:40], stat[:, 40:44]
        ss_mix, r_mix, ss_x1, r_x1 = stat[:, 44:48], stat[:, 48:52], stat[:, 52:56], stat[:, 56:60]
        ss_ff, r_ff = stat[:, 60:68], stat[:, 68:72]
        ss_pool_sb, ss_attn_sum, ss_ff_sum = stat[:, 72:76], stat[:, 76:80], stat[:, 80:84]
        shifted = stat[:, 84:108]

        bank = [ctx.enter_context(nc.psum_tensor(f"bank{i}", [P, HALF], F32)) for i in range(8)]
        S, PT, O, J = bank[0:2], bank[2:4], bank[4:6], bank[6:8]

        rows_dram = nc.dram_tensor("diag_rows_dram", (8, SPAN), F32, kind="Internal").ap()

        x_in = [sem(f"x_in{t}") for t in range(NT)]
        raw_in = [sem(f"raw_in{s}") for s in range(RAW)]
        const_in, row_in, rows_out, bias_in, late_rows_in = (
            sem(n) for n in ("const_in", "row_in", "rows_out", "bias_in", "late_rows_in"))
        y_stored = [sem(f"y_stored{t}") for t in range(NT)]
        pool_const, pool_step = sem("pool_const"), sem("pool_step")
        x_squared, rx_ready, xs_ready, xT_mm, hT_hi, hT_lo = (
            sem(n) for n in ("x_squared", "rx_ready", "xs_ready", "xT_mm", "hT_hi", "hT_lo"))
        vec_mm, vec_ready, diag_mm, diag_copied, wp_hi, wp_lo = (
            sem(n) for n in ("vec_mm", "vec_ready", "diag_mm", "diag_copied", "wp_hi", "wp_lo"))
        flip_mm, bias_ready = sem("flip_mm"), sem("bias_ready")
        split_hi, split_lo = sem("split_hi"), sem("split_lo")
        v_mm, v_hi_done, v_lo_done = sem("v_mm"), sem("v_hi_done"), sem("v_lo_done")
        qk_proj, qk_hi, qk_lo, u_mm, u_copied, u_used, mixed_ready = (
            sem(n) for n in ("qk_proj", "qk_hi", "qk_lo", "u_mm", "u_copied", "u_used", "mixed_ready"))
        score_mm, biased, max_ready, exp_done, pT_mm, pT_hi, pT_lo, inv_ready, pv_mm, y_normed = (
            sem(n) for n in ("score_mm", "biased", "max_ready", "exp_done", "pT_mm", "pT_hi", "pT_lo",
                             "inv_ready", "pv_mm", "y_normed"))
        y_squared, yT_mm, yT_hi, yT_lo = (sem(n) for n in ("y_squared", "yT_mm", "yT_hi", "yT_lo"))
        pm_mm, pm_sq, pm_hi, pm_lo, pool_ss_mm, pool_ss, attn_ss = (
            sem(n) for n in ("pm_mm", "pm_sq", "pm_hi", "pm_lo", "pool_ss_mm", "pool_ss", "attn_ss"))
        rp_ready, ra_ready, outp_mm, outp_scaled, outa_mm, mix_ready = (
            sem(n) for n in ("rp_ready", "ra_ready", "outp_mm", "outp_scaled", "outa_mm", "mix_ready"))
        mix_squared, rm_ready, mix_scaled, x1_ready, x1_squared, r1_ready, xs2_ready = (
            sem(n) for n in ("mix_squared", "rm_ready", "mix_scaled", "x1_ready", "x1_squared", "r1_ready",
                             "xs2_ready"))
        x1T_mm, h2_hi, h2_lo = sem("x1T_mm"), sem("h2_hi"), sem("h2_lo")
        up_mm, relu_done, sq_done, a_hi, a_lo = (sem(n) for n in ("up_mm", "relu_done", "sq_done", "a_hi", "a_lo"))
        down_mm, ff_done, ff_squared, ff_ss, rf_ready, ff_scaled, y_ready = (
            sem(n) for n in ("down_mm", "ff_done", "ff_squared", "ff_ss", "rf_ready", "ff_scaled", "y_ready"))

        def group_col(n):
            return U_ORDER[n]

        block = ctx.enter_context(nc.Block())

        @block.sync
        def _(sp):
            for t in range(NT):
                sp.dma_start(x_tok[:, t, :], x[0, t * P:(t + 1) * P, :]).then_inc(x_in[t], 16)

            w_in_chunks = w_in[0].rearrange("(c p) n -> p c n", p=P)
            w_out_chunks = w_out[0].rearrange("(c p) n -> p c n", p=P)
            w_up_chunks = w_up[0].rearrange("(c p) n -> p c n", p=P)
            w_down_chunks = w_down[0].rearrange("(c p) n -> p c n", p=P)

            def wait_raw_free(d):
                if d >= RAW:
                    sp.wait_ge(split_lo, d - RAW + 1)

            for d in range(2):
                sp.dma_start(raw[:, d, :].rearrange("p (c n) -> p c n", n=HALF),
                             w_in_chunks[:, 4 * d:4 * d + 4, 3 * POOL_W:4 * POOL_W]).then_inc(raw_in[d], 16)
            columns = []
            for n in range(NPAIR):
                columns += [POOL_W + n * P, 2 * POOL_W + n * P, U_ORDER[n] * P]
            for d in range(2, D_WO):
                wait_raw_free(d)
                for e in range(2):
                    c0 = columns[2 * (d - 2) + e]
                    sp.dma_start(raw[:, d % RAW, e * UNIT:(e + 1) * UNIT].rearrange("p (c n) -> p c n", n=P),
                                 w_in_chunks[:, :, c0:c0 + P]).then_inc(raw_in[d % RAW], 16)
            for d in range(D_WO, D_UP):
                wait_raw_free(d)
                c0 = 2 * (d - D_WO)
                sp.dma_start(raw[:, d % RAW, :].rearrange("p (c n) -> p c n", n=D),
                             w_out_chunks[:, c0:c0 + 2, :]).then_inc(raw_in[d % RAW], 16)
            with sp.Fori(0, ND // RAW) as i:
                for s in range(RAW):
                    sp.wait_ge(split_lo, i * RAW + (D_UP + s - RAW + 1))
                    sp.dma_start(raw[:, s, :].rearrange("p (c n) -> p c n", n=2 * P),
                                 w_up_chunks[:, :, ds(i * (RAW * 2 * P) + s * 2 * P, 2 * P)]).then_inc(raw_in[s], 16)
            with sp.Fori(0, ND // RAW) as i:
                for s in range(RAW):
                    sp.wait_ge(split_lo, i * RAW + (D_UP + ND + s - RAW + 1))
                    sp.dma_start(raw[:, s, :].rearrange("p (c n) -> p c n", n=D),
                                 w_down_chunks[:, ds(i * (2 * RAW) + 2 * s, 2), :]).then_inc(raw_in[s], 16)
            for t in range(NT):
                sp.wait_ge(y_ready, t + 1)
                sp.dma_start(out[0, t * P:(t + 1) * P, :], y_out[t % 2]).then_inc(y_stored[t], 16)
            for t in range(NT):
                sp.wait_ge(y_stored[t], 16)

        @block.gpsimd
        def _(pool):
            steps = [0]
            used = [0]

            def link(ins):
                steps[0] += 1
                ins.then_inc(pool_step, 1)
                pool.wait_ge(pool_step, steps[0])

            def diagonal(tile, base, step):
                link(nc.gpsimd.memset(tile[:], 0.0))
                link(nc.gpsimd.affine_select(out=tile[:], in_=tile[:], compare_op=ALU.not_equal, fill=1.0, base=base,
                                             pattern=[[step, P]], channel_multiplier=1))

            diagonal(ident, 0, -1)
            diagonal(reverse, -(P - 1), 1)
            link(nc.gpsimd.memset(rel_tab[BUCKETS:BUCKETS + 1, :], MASKED))
            link(nc.gpsimd.memset(zero16[:], 0.0))
            link(nc.gpsimd.memset(ones[:], 1.0))
            link(nc.gpsimd.memset(nhalf[:], -0.5))
            pool.sem_inc(pool_const, 1)

            def rsqrt(dst, src, n, scale, eps):
                v = shifted[:, used[0]:used[0] + n]
                used[0] += n
                link(nc.gpsimd.tensor_scalar(v, src, scale, eps, ALU.mult, ALU.add))
                return nc.gpsimd.tensor_tensor(dst, v, nhalf[:, 0:n], ALU.pow)

            for t in range(NT):
                pool.wait_ge(x_squared, t + 1)
                rsqrt(r_x[:, t:t + 1], ss_x[:, t:t + 1], 1, 1.0 / D, EPS).then_inc(rx_ready, 1)

            for n in range(NG):
                g = group_col(n)
                w = WINDOWS[g]
                pool.wait_ge(u_copied, n + 1)
                if n == 0:
                    nc.gpsimd.memset(u_pad[:, 0:PAD], 0.0)
                    nc.gpsimd.memset(win_a[:, 0:PAD], 0.0)
                    link(nc.gpsimd.memset(win_b[:, 0:PAD], 0.0))
                    pool.wait_ge(const_in, 16 * 7)
                else:
                    pool.wait_ge(mixed_ready, n)
                src, dst, other, step = u_pad, win_a, win_b, 1
                while step < w:
                    link(nc.gpsimd.tensor_tensor(dst[:, PAD:], src[:, PAD:], src[:, PAD - step:PAD + SEQ - step],
                                                 ALU.add))
                    src, dst, other, step = dst, other, dst, 2 * step
                link(nc.gpsimd.tensor_tensor(src[:, PAD:2 * PAD], src[:, PAD:2 * PAD], ratio[:, g, :], ALU.mult))
                link(nc.gpsimd.tensor_scalar(src[:, PAD:], src[:, PAD:], 1.0 / w, None, ALU.mult))
                link(nc.gpsimd.tensor_tensor(dst[:, PAD:], src[:, PAD:], u_pad[:, PAD:], ALU.subtract))
                pool.sem_inc(u_used, 1)
                link(nc.gpsimd.tensor_copy(mixed[n][:, 0, :], dst[:, PAD:]))
                nc.gpsimd.tensor_tensor(mixed[n][:, 1, :], dst[:, PAD:], mixed[n][:, 0, :],
                                        ALU.subtract).then_inc(mixed_ready, 1)

            pool.wait_ge(pool_ss, 1)
            rsqrt(r_pool, ss_pool_sb, NT, WS * WS / POOL_W, WS * WS * EPS).then_inc(rp_ready, 1)
            pool.wait_ge(attn_ss, 1)
            rsqrt(r_attn, ss_attn_sum, NT, WS * WS / POOL_W, WS * WS * EPS).then_inc(ra_ready, 1)
            for t in range(NT):
                pool.wait_ge(mix_squared, t + 1)
                rsqrt(r_mix[:, t:t + 1], ss_mix[:, t:t + 1], 1, 1.0 / D, EPS).then_inc(rm_ready, 1)
                pool.wait_ge(x1_squared, t + 1)
                rsqrt(r_x1[:, t:t + 1], ss_x1[:, t:t + 1], 1, 1.0 / D, EPS).then_inc(r1_ready, 1)
            for t in range(NT):
                pool.wait_ge(ff_squared, 2 * (t + 1))
                link(nc.gpsimd.tensor_tensor(ss_ff_sum[:, t:t + 1], ss_ff[:, 2 * t:2 * t + 1],
                                             ss_ff[:, 2 * t + 1:2 * t + 2], ALU.add))
                rsqrt(r_ff[:, t:t + 1], ss_ff_sum[:, t:t + 1], 1, 1.0 / D, WS * WS * EPS).then_inc(rf_ready, 1)

        def split_dst(d, part):
            if d < D_WO:
                return big[:, 2 * d:2 * d + 2, part, :]
            if d < D_UP:
                return wo[:, 2 * (d - D_WO):2 * (d - D_WO) + 2, part, :]
            r = 2 * (d % 2)
            return ring[:, r:r + 2, part, :]

        def raw_halves(d):
            return raw[:, d % RAW, :].rearrange("p (s n) -> p s n", s=2)

        def split_hi_op(act, d, i=0):
            act.wait_ge(raw_in[d % RAW], i * 16 + loads_until(d))
            nc.scalar.activation(split_dst(d, 0), raw_halves(d), ACT.Copy, scale=WS).then_inc(split_hi, 1)

        def split_lo_op(dve, d, i=0):
            dve.wait_ge(split_hi, i * RAW + (d + 1))
            nc.vector.scalar_tensor_tensor(out=split_dst(d, 1), in0=raw_halves(d), scalar=WS, in1=split_dst(d, 0),
                                           op0=ALU.mult, op1=ALU.subtract).then_inc(split_lo, 1)

        @block.scalar
        def _(act):
            act.dma_start(row_pre, bass.AP(g_mix_pre.tensor, g_mix_pre.offset, [[0, P], [1, D]])).then_inc(row_in, 16)
            act.dma_start(vec_rows[0:NG, :], pool_scale.rearrange("a (g n) -> (a g) n", n=P)).then_inc(const_in, 16)
            act.dma_start(vec_rows[NG:2 * NG, :], g_pool_out.rearrange("a (g n) -> (a g) n", n=P)).then_inc(const_in, 16)
            act.dma_start(vec_rows[2 * NG:3 * NG, :], g_attn_out.rearrange("a (g n) -> (a g) n", n=P)).then_inc(const_in, 16)
            act.dma_start(rel_tab[0:BUCKETS, :], rel_bias).then_inc(const_in, 16)
            act.dma_start(onehot, bucket_rows).then_inc(const_in, 16)
            act.dma_start(wp_raw.rearrange("p (g n) -> p g n", g=NG), w_pool[0].rearrange("g c n -> c g n")).then_inc(const_in, 16)
            act.dma_start(ratio[:, :, :].rearrange("p g n -> p (g n)"),
                          bass.AP(edge_ratio.tensor, edge_ratio.offset, [[0, P], [1, NG * PAD]])).then_inc(const_in, 16)
            for t in range(NT):
                act.wait_ge(x_in[t], 16)
                if t >= 1:
                    act.wait_ge(x_squared, t)
                nc.scalar.activation(junk0, x_tok[:, t, :], ACT.Square,
                                     accum_out=ss_x[:, t:t + 1]).then_inc(x_squared, 1)
            act.wait_ge(const_in, 16 * 7)
            nc.scalar.activation(wp[:, 0, :, :].rearrange("p g n -> p (g n)"), wp_raw, ACT.Copy,
                                 scale=WS).then_inc(wp_hi, 1)
            act.wait_ge(diag_copied, 1)
            act.dma_start(rows_dram, diag_row).then_inc(rows_out, 16)
            act.wait_ge(rows_out, 16)
            act.dma_start(windows.rearrange("p (h n) -> p h n", n=NEAR),
                          bass.AP(rows_dram.tensor, 0, [[1, P], [SPAN, 8], [1, NEAR]])).then_inc(bias_in, 16)
            for c in range(KC):
                act.wait_ge(xT_mm, c + 1)
                nc.scalar.activation(hT[:, 0, c, :], bank[c][:], ACT.Copy).then_inc(hT_hi, 1)
            for d in range(D_WO):
                if d == D_WO - 1:
                    act.wait_ge(wp_lo, 1)
                    act.wait_ge(diag_mm, 1)
                    act.wait_ge(vec_ready, 1)
                split_hi_op(act, d)
            for t in range(NT):
                act.wait_ge(v_mm, t + 1)
                nc.scalar.activation(v_hi[:, t, :], bank[t][:], ACT.Copy, scale=1 / WS).then_inc(v_hi_done, 1)
            for f in range(4):
                act.wait_ge(flip_mm, f + 1)
                nc.scalar.activation(bias[:, f * HALF:(f + 1) * HALF], O[f % 2][:], ACT.Copy).then_inc(bias_ready, 1)
            for d in range(D_WO, D_UP):
                split_hi_op(act, d)

            def qk_parts(p):
                act.wait_ge(qk_proj, 2 * p + 2)
                nc.scalar.activation(kT[:, 0, :], J[0][:], ACT.Copy, scale=1 / WS).then_inc(qk_hi, 1)
                nc.scalar.activation(qT[:, 0, :], J[1][:], ACT.Copy, scale=1 / WS / 8).then_inc(qk_hi, 1)

            def exp_step(p, s):
                n = (s % NT + 1) * P
                act.wait_ge(max_ready, p * STEPS + (s + 1))
                if s >= 2:
                    act.wait_ge(pT_mm, p * STEPS + (s - 1))
                c = s % 4
                nc.scalar.activation(prob[s % 2][:, 0:n], S[s % 2][:, 0:n], ACT.Exp, bias=neg_max[:, c:c + 1],
                                     accum_out=row_sum[:, c:c + 1]).then_inc(exp_done, 1)

            def pair(p, last):
                exp_step(p, 0)
                act.wait_ge(u_mm, p + 1)
                nc.scalar.activation(u_pad[:, PAD:], J[0][:], ACT.Copy, scale=1 / WS).then_inc(u_copied, 1)
                for s in range(STEPS):
                    if s + 1 < STEPS:
                        exp_step(p, s + 1)
                    n = (s % NT + 1) * P
                    act.wait_ge(pT_mm, p * STEPS + (s + 1))
                    if s >= 2:
                        act.wait_ge(pv_mm, p * STEPS + (s - 1))
                    nc.scalar.activation(pT[s % 2][:, 0, 0:n], PT[s % 2][:, 0:n], ACT.Copy).then_inc(pT_hi, 1)
                if not last:
                    act.wait_ge(score_mm, p * STEPS + STEPS)
                    qk_parts(p + 1)
                act.wait_ge(y_normed, p * STEPS + STEPS)
                for t in range(NT):
                    ins = nc.scalar.activation(junk1[:, t * P:(t + 1) * P], y_tok[:, t, :], ACT.Square,
                                               accum_out=ss_attn[:, ds(p * NT + t, 1)])
                ins.then_inc(y_squared, 1)
                act.wait_ge(yT_mm, p + 1)
                y_chunk = flat[:, ds(p * UNIT, SEQ)]
                nc.scalar.activation(y_chunk, PT[0][:], ACT.Copy,
                                     scale=vecs[:, ds(p + 2 * NG, 1)]).then_inc(yT_hi, 1)
                act.wait_ge(y_squared, p + 1)
                act.wait_ge(u_used, p + 1)

            qk_parts(0)
            with act.Fori(0, NPAIR - 1) as p:
                pair(p, False)
            pair(NPAIR - 1, True)

            for n in range(NG):
                g = group_col(n)
                act.wait_ge(pm_mm, n + 1)
                act.wait_ge(vec_ready, 1)
                nc.scalar.activation(sq_pool[:, n * SEQ:(n + 1) * SEQ], J[n % 2][:], ACT.Square,
                                     scale=vecs[:, 3 * NG + g:3 * NG + g + 1]).then_inc(pm_sq, 1)
                nc.scalar.activation(y_half(SLOT_YP, g)[:, 0, :], J[n % 2][:], ACT.Copy,
                                     scale=vecs[:, 4 * NG + g:4 * NG + g + 1]).then_inc(pm_hi, 1)
            act.wait_ge(rp_ready, 1)
            for g in range(2 * NT):
                t, h = g // 2, g % 2
                act.wait_ge(outp_mm, g + 1)
                nc.scalar.activation(mix(t)[:, h * HALF:(h + 1) * HALF], J[g % 2][:], ACT.Copy,
                                     scale=r_pool[:, t:t + 1]).then_inc(outp_scaled, 1)

            act.dma_start(row_mix_post, bass.AP(g_mix_post.tensor, g_mix_post.offset, [[0, P], [1, D]])).then_inc(late_rows_in, 16)
            act.dma_start(row_mlp_pre, bass.AP(g_mlp_pre.tensor, g_mlp_pre.offset, [[0, P], [1, D]])).then_inc(late_rows_in, 16)
            act.dma_start(row_mlp_post, bass.AP(g_mlp_post.tensor, g_mlp_post.offset, [[0, P], [1, D]])).then_inc(late_rows_in, 16)
            split_hi_op(act, D_UP)
            split_hi_op(act, D_UP + 1)
            for t in range(NT):
                act.wait_ge(mix_ready, 2 * (t + 1))
                if t >= 1:
                    act.wait_ge(x1_squared, t)
                nc.scalar.activation(junk2, mix(t), ACT.Square, accum_out=ss_mix[:, t:t + 1]).then_inc(mix_squared, 1)
                act.wait_ge(x1_ready, t + 1)
                act.wait_ge(mix_squared, t + 1)
                nc.scalar.activation(junk2, x_tok[:, t, :], ACT.Square,
                                     accum_out=ss_x1[:, t:t + 1]).then_inc(x1_squared, 1)
                for h in range(2):
                    act.wait_ge(x1T_mm, 2 * t + h + 1)
                    nc.scalar.activation(hT[:, 0, 4 * h:4 * h + 4, t * P:(t + 1) * P],
                                         J[h][:].rearrange("p (c n) -> p c n", n=P), ACT.Copy).then_inc(h2_hi, 1)

            with act.Fori(0, ND // RAW) as i:
                for dd in range(RAW):
                    for e in range(2):
                        j = 2 * dd + e
                        act.wait_ge(up_mm, i * (2 * RAW) + (j + 1))
                        if j >= 2:
                            act.wait_ge(sq_done, i * (2 * RAW) + (j - 1))
                        nc.scalar.activation(relu[j % 2], bank[j % 4][:], ACT.Relu, scale=1 / WS).then_inc(relu_done, 1)
                        act.wait_ge(relu_done, i * (2 * RAW) + (j + 1))
                        nc.scalar.activation(flat[:, ds(i * (2 * RAW * UNIT) + j * UNIT, SEQ)], relu[j % 2],
                                             ACT.Square).then_inc(a_hi, 1)
                    split_hi_op(act, D_UP + 2 + dd, i)
                act.wait_ge(sq_done, i * (2 * RAW) + 2 * RAW)
            with act.Fori(0, ND // RAW - 1) as i:
                for dd in range(RAW):
                    act.wait_ge(down_mm, i * RAW + (dd + 1))
                    split_hi_op(act, D_UP + ND + 2 + dd, i)
            for dd in range(2):
                act.wait_ge(down_mm, ND - RAW + dd + 1)
                split_hi_op(act, D_UP + 2 * ND - 2 + dd)
            for t in range(NT):
                act.wait_ge(ff_done, t + 1)
                for h in range(2):
                    if 2 * t + h:
                        act.wait_ge(ff_squared, 2 * t + h)
                    nc.scalar.activation(junk2[:, 0:HALF], bank[2 * t + h][:], ACT.Square,
                                         accum_out=ss_ff[:, 2 * t + h:2 * t + h + 1]).then_inc(ff_squared, 1)

        @block.vector
        def _(dve):
            dve.sem_inc(yT_lo, 1)
            dve.wait_ge(diag_mm, 1)
            nc.vector.tensor_copy(diag_row, bank[0][0:8, 0:SPAN]).then_inc(diag_copied, 1)
            dve.wait_ge(vec_mm, 1)
            nc.vector.tensor_copy(vecs[:, 0:3 * NG], bank[1][:, 0:3 * NG]).then_inc(vec_ready, 1)
            dve.wait_ge(vec_ready, 1)
            nc.vector.tensor_scalar(vecs[:, 3 * NG:4 * NG], vecs[:, 0:NG], 1 / WS, None, ALU.mult).then_inc(vec_ready, 1)
            dve.wait_ge(vec_ready, 2)
            nc.vector.tensor_tensor(vecs[:, 4 * NG:5 * NG], vecs[:, 3 * NG:4 * NG], vecs[:, NG:2 * NG],
                                    ALU.mult).then_inc(vec_ready, 1)
            dve.wait_ge(row_in, 16)
            for t in range(NT):
                dve.wait_ge(rx_ready, t + 1)
                nc.vector.scalar_tensor_tensor(out=xs[t], in0=x_tok[:, t, :], scalar=r_x[:, t:t + 1], in1=row_pre,
                                               op0=ALU.mult, op1=ALU.mult).then_inc(xs_ready, 1)
            dve.wait_ge(wp_hi, 1)
            nc.vector.scalar_tensor_tensor(out=wp[:, 1, :, :].rearrange("p g n -> p (g n)"), in0=wp_raw, scalar=WS,
                                           in1=wp[:, 0, :, :].rearrange("p g n -> p (g n)"), op0=ALU.mult,
                                           op1=ALU.subtract).then_inc(wp_lo, 1)
            for c in range(KC):
                dve.wait_ge(hT_hi, c + 1)
                nc.vector.tensor_tensor(hT[:, 1, c, :], bank[c][:], hT[:, 0, c, :], ALU.subtract).then_inc(hT_lo, 1)
            for d in range(D_WO):
                split_lo_op(dve, d)
            for t in range(NT):
                dve.wait_ge(v_hi_done, t + 1)
                nc.vector.scalar_tensor_tensor(out=v_lo[:, t, :], in0=bank[t][:], scalar=1 / WS, in1=v_hi[:, t, :],
                                               op0=ALU.mult, op1=ALU.subtract).then_inc(v_lo_done, 1)
            for d in range(D_WO, D_UP):
                split_lo_op(dve, d)

            def qk_parts(p):
                dve.wait_ge(qk_hi, 2 * p + 1)
                nc.vector.scalar_tensor_tensor(out=kT[:, 1, :], in0=J[0][:], scalar=1 / WS, in1=kT[:, 0, :],
                                               op0=ALU.mult, op1=ALU.subtract).then_inc(qk_lo, 1)
                dve.wait_ge(qk_hi, 2 * p + 2)
                nc.vector.scalar_tensor_tensor(out=qT[:, 1, :], in0=J[1][:], scalar=1 / WS / 8, in1=qT[:, 0, :],
                                               op0=ALU.mult, op1=ALU.subtract).then_inc(qk_lo, 1)

            def max_step(p, s):
                i, h, b = s % NT, s // NT, s % 2
                n = (i + 1) * P
                near = min(NEAR, n)
                dve.wait_ge(score_mm, p * STEPS + (s + 1))
                nc.vector.tensor_tensor(S[b][:, n - near:n], S[b][:, n - near:n],
                                        bias[:, ds(p * (2 * NEAR) + (h * NEAR + NEAR - near), near)],
                                        ALU.add).then_inc(biased, 1)
                dve.wait_ge(biased, p * STEPS + (s + 1))
                c = s % 4
                nc.vector.tensor_reduce(neg_max[:, c:c + 1], S[b][:, 0:n], AX, ALU.max,
                                        negate=True).then_inc(max_ready, 1)

            def norm_step(p, s):
                i, h = s % NT, s // NT
                c = s % 4
                dve.wait_ge(pv_mm, p * STEPS + (s + 1))
                dve.wait_ge(inv_ready, p * STEPS + (s + 1))
                nc.vector.tensor_scalar(y_tok[:, i, h * HD:(h + 1) * HD], O[s % 2][:, 0:HD], row_inv[:, c:c + 1],
                                        None, ALU.mult).then_inc(y_normed, 1)

            def pair(p, last):
                max_step(p, 0)
                for s in range(STEPS):
                    if s + 1 < STEPS:
                        max_step(p, s + 1)
                    n = (s % NT + 1) * P
                    c = s % 4
                    dve.wait_ge(exp_done, p * STEPS + (s + 1))
                    nc.vector.reciprocal(row_inv[:, c:c + 1], row_sum[:, c:c + 1]).then_inc(inv_ready, 1)
                    dve.wait_ge(pT_hi, p * STEPS + (s + 1))
                    nc.vector.tensor_tensor(pT[s % 2][:, 1, 0:n], PT[s % 2][:, 0:n], pT[s % 2][:, 0, 0:n],
                                            ALU.subtract).then_inc(pT_lo, 1)
                    if s >= 1:
                        norm_step(p, s - 1)
                if not last:
                    qk_parts(p + 1)
                norm_step(p, STEPS - 1)
                dve.wait_ge(yT_hi, p + 1)
                dve.wait_ge(y_squared, p + 1)
                nc.vector.scalar_tensor_tensor(out=flat[:, ds(p * UNIT + SEQ, SEQ)], in0=PT[0][:],
                                               scalar=vecs[:, ds(p + 2 * NG, 1)], in1=flat[:, ds(p * UNIT, SEQ)],
                                               op0=ALU.mult, op1=ALU.subtract).then_inc(yT_lo, 1)

            qk_parts(0)
            dve.wait_ge(bias_ready, 4)
            with dve.Fori(0, NPAIR - 1) as p:
                pair(p, False)
            pair(NPAIR - 1, True)

            dve.wait_ge(y_squared, NPAIR)
            nc.vector.tensor_reduce(ss_attn_sum, ss_attn.rearrange("p (c t) -> p t c", c=NPAIR), AX,
                                    ALU.add).then_inc(attn_ss, 1)
            for n in range(NG):
                g = group_col(n)
                dve.wait_ge(pm_hi, n + 1)
                nc.vector.scalar_tensor_tensor(out=y_half(SLOT_YP, g)[:, 1, :], in0=J[n % 2][:],
                                               scalar=vecs[:, 4 * NG + g:4 * NG + g + 1],
                                               in1=y_half(SLOT_YP, g)[:, 0, :], op0=ALU.mult,
                                               op1=ALU.subtract).then_inc(pm_lo, 1)
            dve.wait_ge(pool_ss_mm, 1)
            nc.vector.tensor_copy(ss_pool_sb, J[0][:, 0:NT]).then_inc(pool_ss, 1)

            split_lo_op(dve, D_UP)
            split_lo_op(dve, D_UP + 1)
            dve.wait_ge(ra_ready, 1)
            dve.wait_ge(late_rows_in, 16 * 3)

            def h2_parts(t):
                for h in range(2):
                    dve.wait_ge(h2_hi, 2 * t + h + 1)
                    nc.vector.tensor_tensor(hT[:, 1, 4 * h:4 * h + 4, t * P:(t + 1) * P],
                                            J[h][:].rearrange("p (c n) -> p c n", n=P),
                                            hT[:, 0, 4 * h:4 * h + 4, t * P:(t + 1) * P],
                                            ALU.subtract).then_inc(h2_lo, 1)

            for t in range(NT):
                for h in range(2):
                    dve.wait_ge(outa_mm, 2 * t + h + 1)
                    dve.wait_ge(outp_scaled, 2 * t + h + 1)
                    m = mix(t)[:, h * HALF:(h + 1) * HALF]
                    nc.vector.scalar_tensor_tensor(out=m, in0=bank[(2 * t + h) % 6][:], scalar=r_attn[:, t:t + 1],
                                                   in1=m, op0=ALU.mult, op1=ALU.add).then_inc(mix_ready, 1)
                dve.wait_ge(rm_ready, t + 1)
                nc.vector.scalar_tensor_tensor(out=mix(t), in0=mix(t), scalar=r_mix[:, t:t + 1], in1=row_mix_post,
                                               op0=ALU.mult, op1=ALU.mult).then_inc(mix_scaled, 1)
                dve.wait_ge(mix_scaled, t + 1)
                nc.vector.tensor_tensor(x_tok[:, t, :], x_tok[:, t, :], mix(t), ALU.add).then_inc(x1_ready, 1)
                if t >= 1:
                    h2_parts(t - 1)
                dve.wait_ge(r1_ready, t + 1)
                if t >= 2:
                    dve.wait_ge(x1T_mm, 2 * (t - 1))
                nc.vector.scalar_tensor_tensor(out=xs2[t % 2], in0=x_tok[:, t, :], scalar=r_x1[:, t:t + 1],
                                               in1=row_mlp_pre, op0=ALU.mult, op1=ALU.mult).then_inc(xs2_ready, 1)
            h2_parts(NT - 1)

            with dve.Fori(0, ND // RAW) as i:
                for dd in range(RAW):
                    for e in range(2):
                        j = 2 * dd + e
                        dve.wait_ge(relu_done, i * (2 * RAW) + (j + 1))
                        if j >= 2:
                            dve.wait_ge(a_lo, i * (2 * RAW) + (j - 1))
                        nc.vector.tensor_tensor(squared[j % 2], relu[j % 2], relu[j % 2], ALU.mult).then_inc(sq_done, 1)
                        dve.wait_ge(sq_done, i * (2 * RAW) + (j + 1))
                        dve.wait_ge(a_hi, i * (2 * RAW) + (j + 1))
                        nc.vector.tensor_tensor(flat[:, ds(i * (2 * RAW * UNIT) + (j * UNIT + SEQ), SEQ)],
                                                squared[j % 2],
                                                flat[:, ds(i * (2 * RAW * UNIT) + j * UNIT, SEQ)],
                                                ALU.subtract).then_inc(a_lo, 1)
                    split_lo_op(dve, D_UP + 2 + dd, i)
                dve.wait_ge(a_lo, i * (2 * RAW) + 2 * RAW)
            with dve.Fori(0, ND // RAW - 1) as i:
                for dd in range(RAW):
                    split_lo_op(dve, D_UP + ND + 2 + dd, i)
            for dd in range(2):
                split_lo_op(dve, D_UP + 2 * ND - 2 + dd)

            for t in range(NT):
                dve.wait_ge(rf_ready, t + 1)
                if t >= 2:
                    dve.wait_ge(y_stored[t - 2], 16)
                for h in range(2):
                    cols = slice(h * HALF, (h + 1) * HALF)
                    nc.vector.scalar_tensor_tensor(out=y_out[t % 2][:, cols], in0=bank[2 * t + h][:],
                                                   scalar=r_ff[:, t:t + 1], in1=row_mlp_post[:, cols], op0=ALU.mult,
                                                   op1=ALU.mult).then_inc(ff_scaled, 1)
                dve.wait_ge(ff_scaled, 2 * (t + 1))
                nc.vector.tensor_tensor(y_out[t % 2], y_out[t % 2], x_tok[:, t, :], ALU.add).then_inc(y_ready, 1)

        @block.tensor
        def _(pe):
            def passes(dst, w_hi, w_lo, m_hi, m_lo, first, final):
                nc.tensor.matmul(dst, w_hi, m_hi, start=first, stop=False)
                nc.tensor.matmul(dst, w_hi, m_lo, start=False, stop=False)
                return nc.tensor.matmul(dst, w_lo, m_hi, start=False, stop=final)

            pe.wait_ge(const_in, 16 * 7)
            pe.wait_ge(pool_const, 1)
            nc.tensor.matmul(bank[0][0:8, 0:SPAN], rel_tab, onehot, start=True, stop=True).then_inc(diag_mm, 1)
            nc.tensor.transpose(bank[1][:, 0:3 * NG], vec_rows, ident[0:3 * NG, 0:3 * NG]).then_inc(vec_mm, 1)
            pe.wait_ge(diag_copied, 1)
            pe.wait_ge(vec_ready, 1)
            for t in range(NT):
                pe.wait_ge(xs_ready, t + 1)
                for c in range(KC):
                    ins = nc.tensor.transpose(bank[c][:, t * P:(t + 1) * P], xs[t][:, c * P:(c + 1) * P], ident[:])
                    if t == NT - 1:
                        ins.then_inc(xT_mm, 1)
            for c in range(KC):
                pe.wait_ge(hT_lo, max(c + 1, NT))
                if c % 4 == 0:
                    pe.wait_ge(split_lo, c // 4 + 1)
                w = big[:, SLOT_V + c // 2, :, (c % 2) * HALF:(c % 2) * HALF + HALF]
                for t in range(NT):
                    ins = passes(bank[t][:], hT[:, 0, c, t * P:(t + 1) * P], hT[:, 1, c, t * P:(t + 1) * P],
                                 w[:, 0, :], w[:, 1, :], c == 0, c == KC - 1)
                    if c == KC - 1:
                        ins.then_inc(v_mm, 1)

            def project(dst, slot, chunks):
                for c in chunks:
                    ins = passes(dst, flat[:, ds(slot * (2 * UNIT) + c * P, P)],
                                 flat[:, ds(slot * (2 * UNIT) + (UNIT + c * P), P)],
                                 hT[:, 0, c, :], hT[:, 1, c, :], c == 0, c == KC - 1)
                return ins

            def scores(p, s):
                i, h, b = s % NT, s // NT, s % 2
                n = (i + 1) * P
                if s >= 2:
                    pe.wait_ge(exp_done, p * STEPS + (s - 1))
                rows = slice(h * HD, (h + 1) * HD)
                passes(S[b][:, 0:n], qT[rows, 0, i * P:(i + 1) * P], qT[rows, 1, i * P:(i + 1) * P],
                       kT[rows, 0, 0:n], kT[rows, 1, 0:n], True, True).then_inc(score_mm, 1)

            def transpose_probs(p, s):
                pe.wait_ge(exp_done, p * STEPS + (s + 1))
                if s == 0:
                    pe.wait_ge(yT_lo, p + 1)
                for j in range(s % NT + 1):
                    ins = nc.tensor.transpose(PT[s % 2][:, j * P:(j + 1) * P], prob[s % 2][:, j * P:(j + 1) * P],
                                              ident[:])
                ins.then_inc(pT_mm, 1)

            def outputs(p, s):
                i, h, b = s % NT, s // NT, s % 2
                pe.wait_ge(pT_lo, p * STEPS + (s + 1))
                if s >= 2:
                    pe.wait_ge(y_normed, p * STEPS + (s - 1))
                for j in range(i + 1):
                    cols = ds(p * P + h * HD, HD)
                    ins = passes(O[b][:, 0:HD], pT[b][:, 0, j * P:(j + 1) * P], pT[b][:, 1, j * P:(j + 1) * P],
                                 v_hi[:, j, cols], v_lo[:, j, cols], j == 0, j == i)
                ins.then_inc(pv_mm, 1)

            def fill(p, s):
                if s < 3:
                    ins = project(J[1][:], p * 3 + (SLOT_Q + 3), (range(0, 3), range(3, 6), range(6, 8))[s])
                    if s == 2:
                        ins.then_inc(qk_proj, 1)
                elif s < 6:
                    if s == 3:
                        pe.wait_ge(u_copied, p + 1)
                    ins = project(J[0][:], p * 3 + (SLOT_K + 3), (range(0, 3), range(3, 6), range(6, 8))[s - 3])
                    if s == 5:
                        ins.then_inc(qk_proj, 1)

            def pair(p, last):
                pe.wait_ge(qk_lo, p * 2 + 2)
                scores(p, 0)
                scores(p, 1)
                project(J[0][:], p * 3 + SLOT_U, range(4, 8)).then_inc(u_mm, 1)
                for s in range(STEPS):
                    transpose_probs(p, s)
                    if s + 2 < STEPS:
                        scores(p, s + 2)
                    if not last:
                        fill(p, s)
                    outputs(p, s)
                if not last:
                    pe.wait_ge(qk_lo, p * 2 + 3)
                    project(J[0][:], p * 3 + (SLOT_U + 3), range(0, 4))
                pe.wait_ge(y_normed, p * STEPS + STEPS)
                for t in range(NT):
                    ins = nc.tensor.transpose(PT[0][:, t * P:(t + 1) * P], y_tok[:, t, :], ident[:])
                ins.then_inc(yT_mm, 1)

            pe.wait_ge(bias_in, 16)
            pe.wait_ge(hT_lo, KC)
            for f in range(4):
                if f >= 2:
                    pe.wait_ge(bias_ready, f - 1)
                nc.tensor.matmul(O[f % 2][:], reverse[:], windows[:, f * HALF:(f + 1) * HALF], start=True,
                                 stop=True).then_inc(flip_mm, 1)
            pe.wait_ge(split_lo, 3)
            project(J[1][:], SLOT_Q, range(KC)).then_inc(qk_proj, 1)
            project(J[0][:], SLOT_K, range(KC)).then_inc(qk_proj, 1)
            pe.wait_ge(split_lo, D_WO)
            pe.wait_ge(v_lo_done, NT)
            pe.wait_ge(qk_lo, 1)
            project(J[0][:], SLOT_U, range(0, 4))
            with pe.Fori(0, NPAIR - 1) as p:
                pair(p, False)
            pair(NPAIR - 1, True)

            pe.wait_ge(wp_lo, 1)
            pe.wait_ge(u_copied, NG)
            for n in range(NG):
                g = group_col(n)
                pe.wait_ge(mixed_ready, n + 1)
                if n >= 2:
                    pe.wait_ge(pm_lo, n - 1)
                passes(J[n % 2][:], wp[:, 0, g, :], wp[:, 1, g, :], mixed[n][:, 0, :], mixed[n][:, 1, :], True,
                       True).then_inc(pm_mm, 1)
            pe.wait_ge(pm_sq, NG)
            pe.wait_ge(pm_lo, NG)
            for t in range(NT):
                for n in range(NG):
                    ins = nc.tensor.matmul(J[0][:, t:t + 1], sq_pool[:, n * SEQ + t * P:n * SEQ + (t + 1) * P], ones[:],
                                           start=(n == 0), stop=(n == NG - 1))
            ins.then_inc(pool_ss_mm, 1)

            def out_project(dst, slot, first_chunk, t, h):
                for c in range(NG):
                    y = y_half(slot, c)
                    w = wo[:, first_chunk + c, :, h * HALF:(h + 1) * HALF]
                    ins = passes(dst, y[:, 0, t * P:(t + 1) * P], y[:, 1, t * P:(t + 1) * P], w[:, 0, :], w[:, 1, :],
                                 c == 0, c == NG - 1)
                return ins

            pe.wait_ge(split_lo, D_UP)
            for g in range(2 * NT):
                if g == 0:
                    pe.wait_ge(pool_ss, 1)
                if g >= 2:
                    pe.wait_ge(outp_scaled, g - 1)
                out_project(J[g % 2][:], SLOT_YP, 0, g // 2, g % 2).then_inc(outp_mm, 1)

            pe.wait_ge(yT_lo, NPAIR + 1)
            def transpose_x1(t):
                pe.wait_ge(xs2_ready, t + 1)
                for h in range(2):
                    if t == 0:
                        pe.wait_ge(outp_scaled, 2 * NT)
                    else:
                        pe.wait_ge(h2_lo, 2 * (t - 1) + h + 1)
                    for c in range(4):
                        ins = nc.tensor.transpose(J[h][:, c * P:(c + 1) * P],
                                                  xs2[t % 2][:, (4 * h + c) * P:(4 * h + c + 1) * P], ident[:])
                    ins.then_inc(x1T_mm, 1)

            for t in range(NT):
                for h in range(2):
                    b = 2 * t + h
                    if b >= 6:
                        pe.wait_ge(mix_ready, b - 5)
                    out_project(bank[b % 6][:], SLOT_YA, NG, t, h).then_inc(outa_mm, 1)
                if t == 2:
                    transpose_x1(0)
            for t in range(1, NT):
                transpose_x1(t)

            pe.wait_ge(h2_lo, 2 * NT)
            pe.wait_ge(mix_ready, 2 * NT)
            with pe.Fori(0, ND // RAW) as i:
                for dd in range(RAW):
                    pe.wait_ge(split_lo, i * RAW + (D_UP + dd + 1))
                    for e in range(2):
                        j = 2 * dd + e
                        r = 2 * (dd % 2)
                        for c in range(KC):
                            cols = slice((c % 4) * 2 * P + e * P, (c % 4) * 2 * P + (e + 1) * P)
                            ins = passes(bank[j % 4][:], ring[:, r + c // 4, 0, cols], ring[:, r + c // 4, 1, cols],
                                         hT[:, 0, c, :], hT[:, 1, c, :], c == 0, c == KC - 1)
                        ins.then_inc(up_mm, 1)

            pe.wait_ge(relu_done, NF)
            for b in range(2 * NT):
                nc.tensor.matmul(bank[b][:, 0:1], zero16[:], zero16[:, 0:1], start=True, stop=False,
                                 skip_group_check=True)

            def down(j, r, tiles):
                for t in tiles:
                    for h in range(2):
                        for part_a, part_w in ((0, 0), (0, 1), (1, 0)):
                            ins = nc.tensor.matmul(bank[2 * t + h][:],
                                                   flat[:, ds(j * UNIT + (part_a * SEQ + t * P), P)],
                                                   ring[:, r, part_w, h * HALF:(h + 1) * HALF], start=False,
                                                   stop=False, skip_group_check=True)
                return ins

            with pe.Fori(0, ND // RAW - 1) as i:
                for dd in range(RAW):
                    pe.wait_ge(split_lo, i * RAW + (D_UP + ND + dd + 1))
                    pe.wait_ge(a_lo, i * (2 * RAW) + (2 * dd + 2))
                    for e in range(2):
                        ins = down(i * (2 * RAW) + (2 * dd + e), 2 * (dd % 2) + e, range(NT))
                    ins.then_inc(down_mm, 1)
            pe.wait_ge(a_lo, NF)
            for dd in range(2):
                pe.wait_ge(split_lo, D_UP + 2 * ND - RAW + dd + 1)
                for e in range(2):
                    ins = down(NF - 2 * RAW + 2 * dd + e, 2 * dd + e, range(NT))
                ins.then_inc(down_mm, 1)
            pe.wait_ge(split_lo, D_UP + 2 * ND)
            for t in range(NT):
                for e in range(4):
                    ins = down(NF - 4 + e, e, [t])
                ins.then_inc(ff_done, 1)


_INS = ['x', 'w_in', 'w_pool', 'pool_scale', 'rel_bias', 'g_mix_pre', 'g_pool_out', 'g_attn_out', 'w_out',
        'g_mix_post', 'g_mlp_pre', 'w_up', 'w_down', 'g_mlp_post']


def _shape_constants():
    import math as _math
    import numpy as _np
    dist = NEAR - 1 - _np.arange(SPAN)
    exact = BUCKETS // 2
    far = _np.log(_np.maximum(dist, exact).astype(_np.float32) / _np.float32(exact)) / _np.float32(_math.log(8.0))
    bucket = _np.where(dist < exact, _np.maximum(dist, 0),
                       _np.minimum(exact + (far * _np.float32(BUCKETS - exact)).astype(_np.int32), BUCKETS - 1))
    rows = _np.zeros((BUCKETS + 1, SPAN), _np.float32)
    rows[bucket, _np.arange(SPAN)] = 1.0
    rows[BUCKETS - 1] -= 1.0
    rows[BUCKETS] = dist < 0
    ratio = _np.array([[w / min(t + 1, w) for t in range(PAD)] for w in WINDOWS], _np.float32).reshape(1, -1)
    return rows, ratio


def kernel(**inputs):
    import numpy as _np
    import concourse.bacc as _bacc
    from concourse import mybir as _mybir
    from concourse.bass_utils import run_bass_kernel_spmd as _run

    nc = _bacc.Bacc("TRN2", target_bir_lowering=False, num_devices=1)
    rows, ratio = _shape_constants()
    arrays, args = {}, []
    for name, a in [(n, inputs[n]) for n in _INS] + [("bucket_rows", rows), ("edge_ratio", ratio)]:
        a = _np.ascontiguousarray(a)
        arrays[f"in_{name}_dram"] = a
        args.append(nc.dram_tensor(f"in_{name}_dram", a.shape, _mybir.dt.from_np(a.dtype), kind="ExternalInput").ap())
    args.append(nc.dram_tensor("out_0_dram", (1, SEQ, D), _mybir.dt.float32, kind="ExternalOutput").ap())
    hybrid_layer(nc, *args)
    r = _run(nc, [arrays], core_ids=[0])
    return r.results[0]["out_0_dram"]
```

```python
from contextlib import ExitStack

import concourse.bass as bass
from concourse import mybir

F32 = mybir.dt.float32
F16 = mybir.dt.float16
ALU = mybir.AluOpType
ACT = mybir.ActivationFunctionType
AX = mybir.AxisListType.X
ds = bass.ds

P = 128
SEQ, D = 512, 1024
NT = SEQ // P
KC = D // P
HALF = 512
POOL_W = D // 2
WINDOWS = (2, 4, 8, 16)
NG = len(WINDOWS)
PAD = max(WINDOWS)
HD = 64
NPAIR = POOL_W // P
STEPS = 2 * NT
D_FF = 4 * D
NF = D_FF // P
BUCKETS = 32
NEAR = 2 * P
SPAN = 3 * P
WS = 32.0
EPS = 1e-6
MASKED = -1e30
UNIT = 1024
RAW = 4

SLOT_V = 0
SLOT_Q, SLOT_K, SLOT_U = 4, 5, 6
U_ORDER = (3, 0, 1, 2)
SLOT_YA, SLOT_YP = 0, 4
SLOT_SQ = 2
SLOT_MIX = (7, 8, 10, 11)
D_WO, D_UP = 8, 12
ND = NF // 2


def loads_until(d):
    return sum(32 if 2 <= e < D_WO else 16 for e in range(d % RAW, d + 1, RAW))


def hybrid_layer(nc, x, w_in, w_pool, pool_scale, rel_bias, g_mix_pre, g_pool_out, g_attn_out,
                 w_out, g_mix_post, g_mlp_pre, w_up, w_down, g_mlp_post, bucket_rows, edge_table, out):
    ctx = ExitStack()
    with ctx:
        def sb(name, shape, dt=F32):
            return ctx.enter_context(nc.sbuf_tensor(name, shape, dt))

        def sem(name):
            return ctx.enter_context(nc.semaphore(name))

        x_tok = sb("x_tok", [P, NT, D])
        hT = sb("hT", [P, 2, KC, SEQ], F16)
        raw = sb("raw", [P, RAW, 2 * UNIT])
        big = sb("big", [P, 16, 2, UNIT], F16)
        wo = sb("wo", [P, KC, 2, UNIT], F16)
        ring = sb("ring", [P, 4, 2, UNIT], F16)
        scr = sb("scr", [P, 6144])
        ident = sb("ident", [P, P])
        reverse = sb("reverse", [P, P])
        ones = sb("ones", [P, 1])
        nhalf = sb("nhalf", [P, NT])
        edges = sb("edges", [P, NG * PAD + NG])
        wp = sb("wp", [P, 2, NG, P], F16)
        vecs = sb("vecs", [P, 5 * NG])
        zero16 = sb("zero16", [P, P], F16)
        stat = sb("stat", [P, 112])

        flat = big[:, :, :, :].rearrange("p s a n -> p (s a n)")
        aT = flat.rearrange("p (j a n) -> p j a n", j=NF, a=2)
        v_hi = ring[:, 0, :, :].rearrange("p a (t n) -> p (a t) n", n=HALF)
        v_lo = ring[:, 1, :, :].rearrange("p a (t n) -> p (a t) n", n=HALF)
        bias = ring[:, 2:4, :, :].rearrange("p s a n -> p (s a n)").bitcast(F32)
        late = wo[:, 2:4, :, :].rearrange("p s a n -> p (s a n)").bitcast(F32)
        onehot, diag_row, wp_raw = late[0:BUCKETS + 1, 0:SPAN], late[0:8, 384:384 + SPAN], late[:, 1024:1536]
        vec_rows, rel_tab = late[0:3 * NG, 768:896], late[0:BUCKETS + 1, 896:904]

        def mix(t):
            return big[:, SLOT_MIX[t], :, :].rearrange("p a n -> p (a n)").bitcast(F32)

        def y_half(slot, c):
            return big[:, slot + c // 2, c % 2, :].rearrange("p (a n) -> p a n", a=2)

        sq_pool = big[:, SLOT_SQ:SLOT_SQ + 2, :, :].rearrange("p s a n -> p (s a n)").bitcast(F32)
        mixed = [big[:, SLOT_U + 3 * n, 0, :].rearrange("p (a n) -> p a n", a=2) for n in range(NG)]

        xs = [scr[:, UNIT * t:UNIT * (t + 1)] for t in range(NT)]
        row_pre, junk0 = scr[:, 4096:5120], scr[:, 5120:6144]
        windows = scr[:, 0:2048]
        prob = [scr[:, 0:512], scr[:, 512:1024]]
        pT = [scr[:, 1024 + 512 * b:1536 + 512 * b].bitcast(F16).rearrange("p (a n) -> p a n", a=2) for b in range(2)]
        qT = scr[:, 2048:2560].bitcast(F16).rearrange("p (a n) -> p a n", a=2)
        kT = scr[:, 2560:3072].bitcast(F16).rearrange("p (a n) -> p a n", a=2)
        u_pad, win_a, win_b = (scr[:, 3072 + 528 * n:3600 + 528 * n] for n in range(3))
        y_tok = scr[:, 4656:5168].rearrange("p (t n) -> p t n", t=NT)
        junk1 = scr[:, 5168:5680]
        xs2 = [scr[:, 0:1024], scr[:, 1024:2048]]
        row_mix_post, row_mlp_pre, junk2, row_mlp_post = (scr[:, 2048 + 1024 * n:3072 + 1024 * n] for n in range(4))
        relu = [scr[:, 0:512], scr[:, 512:1024]]
        squared = [scr[:, 1024:1536], scr[:, 1536:2048]]
        y_out = [scr[:, 0:1024], scr[:, 1024:2048]]

        ss_x, r_x = stat[:, 0:4], stat[:, 4:8]
        neg_max, row_sum, row_inv = stat[:, 8:12], stat[:, 12:16], stat[:, 16:20]
        ss_attn = stat[:, 20:36]
        r_pool, r_attn = stat[:, 36:40], stat[:, 40:44]
        ss_mix, r_mix, ss_x1, r_x1 = stat[:, 44:48], stat[:, 48:52], stat[:, 52:56], stat[:, 56:60]
        ss_ff, r_ff = stat[:, 60:68], stat[:, 68:72]
        ss_pool_sb, ss_attn_sum, ss_ff_sum = stat[:, 72:76], stat[:, 76:80], stat[:, 80:84]
        shifted = stat[:, 84:108]

        bank = [ctx.enter_context(nc.psum_tensor(f"bank{i}", [P, HALF], F32)) for i in range(8)]
        S, PT, O, J = bank[0:2], bank[2:4], bank[4:6], bank[6:8]

        rows_dram = nc.dram_tensor("diag_rows_dram", (8, SPAN), F32, kind="Internal").ap()

        x_in = [sem(f"x_in{t}") for t in range(NT)]
        raw_in = [sem(f"raw_in{s}") for s in range(RAW)]
        const_in, row_in, rows_out, bias_in, late_rows_in = (
            sem(n) for n in ("const_in", "row_in", "rows_out", "bias_in", "late_rows_in"))
        y_stored = [sem(f"y_stored{t}") for t in range(NT)]
        pool_const, pool_step = sem("pool_const"), sem("pool_step")
        x_squared, rx_ready, xs_ready, xT_mm, hT_hi, hT_lo = (
            sem(n) for n in ("x_squared", "rx_ready", "xs_ready", "xT_mm", "hT_hi", "hT_lo"))
        vec_mm, vec_ready, diag_mm, diag_copied, wp_hi, wp_lo = (
            sem(n) for n in ("vec_mm", "vec_ready", "diag_mm", "diag_copied", "wp_hi", "wp_lo"))
        flip_mm, bias_ready = sem("flip_mm"), sem("bias_ready")
        split_hi, split_lo = sem("split_hi"), sem("split_lo")
        v_mm, v_hi_done, v_lo_done = sem("v_mm"), sem("v_hi_done"), sem("v_lo_done")
        qk_proj, qk_hi, qk_lo, u_mm, u_copied, window_ready, pooled, mixed_hi, mixed_ready = (
            sem(n) for n in ("qk_proj", "qk_hi", "qk_lo", "u_mm", "u_copied", "window_ready", "pooled", "mixed_hi",
                             "mixed_ready"))
        table_loaded, pad_ready = sem("table_loaded"), sem("pad_ready")
        score_mm, biased, max_ready, exp_done, pT_mm, pT_hi, pT_lo, inv_ready, pv_mm, y_normed = (
            sem(n) for n in ("score_mm", "biased", "max_ready", "exp_done", "pT_mm", "pT_hi", "pT_lo",
                             "inv_ready", "pv_mm", "y_normed"))
        y_squared, yT_mm, yT_hi, yT_lo = (sem(n) for n in ("y_squared", "yT_mm", "yT_hi", "yT_lo"))
        pm_mm, pm_sq, pm_hi, pm_lo, pool_ss_mm, pool_ss, attn_ss = (
            sem(n) for n in ("pm_mm", "pm_sq", "pm_hi", "pm_lo", "pool_ss_mm", "pool_ss", "attn_ss"))
        rp_ready, ra_ready, outp_mm, outp_scaled, outa_mm, mix_ready = (
            sem(n) for n in ("rp_ready", "ra_ready", "outp_mm", "outp_scaled", "outa_mm", "mix_ready"))
        mix_squared, rm_ready, mix_scaled, x1_ready, x1_squared, r1_ready, xs2_ready = (
            sem(n) for n in ("mix_squared", "rm_ready", "mix_scaled", "x1_ready", "x1_squared", "r1_ready",
                             "xs2_ready"))
        x1T_mm, h2_hi, h2_lo = sem("x1T_mm"), sem("h2_hi"), sem("h2_lo")
        up_mm, relu_done, sq_done, a_hi, a_lo = (sem(n) for n in ("up_mm", "relu_done", "sq_done", "a_hi", "a_lo"))
        down_mm, ff_done, ff_squared, ff_ss, rf_ready, ff_scaled, y_ready = (
            sem(n) for n in ("down_mm", "ff_done", "ff_squared", "ff_ss", "rf_ready", "ff_scaled", "y_ready"))

        out_groups = [(br, t, h) for br, t in (("pool", 0), ("pool", 1), ("attn", 0), ("attn", 1), ("pool", 2),
                                               ("attn", 2), ("pool", 3), ("attn", 3)) for h in range(2)]

        def out_bank(br, t, h):
            return bank[(0, 1, 4, 5, 3, 2)[out_groups.index((br, t, h)) % 6]]

        block = ctx.enter_context(nc.Block())

        @block.sync
        def _(sp):
            for t in range(NT):
                sp.dma_start(x_tok[:, t, :], x[0, t * P:(t + 1) * P, :]).then_inc(x_in[t], 16)

            w_in_chunks = w_in[0].rearrange("(c p) n -> p c n", p=P)
            w_out_chunks = w_out[0].rearrange("(c p) n -> p c n", p=P)
            w_up_chunks = w_up[0].rearrange("(c p) n -> p c n", p=P)
            w_down_chunks = w_down[0].rearrange("(c p) n -> p c n", p=P)

            def wait_raw_free(d):
                if d >= RAW:
                    sp.wait_ge(split_lo, d - RAW + 1)

            for d in range(2):
                sp.dma_start(raw[:, d, :].rearrange("p (c n) -> p c n", n=HALF),
                             w_in_chunks[:, 4 * d:4 * d + 4, 3 * POOL_W:4 * POOL_W]).then_inc(raw_in[d], 16)
            columns = []
            for n in range(NPAIR):
                columns += [POOL_W + n * P, 2 * POOL_W + n * P, U_ORDER[n] * P]
            for d in range(2, D_WO):
                wait_raw_free(d)
                for e in range(2):
                    c0 = columns[2 * (d - 2) + e]
                    sp.dma_start(raw[:, d % RAW, e * UNIT:(e + 1) * UNIT].rearrange("p (c n) -> p c n", n=P),
                                 w_in_chunks[:, :, c0:c0 + P]).then_inc(raw_in[d % RAW], 16)
            for d in range(D_WO, D_UP):
                wait_raw_free(d)
                c0 = 2 * (d - D_WO)
                sp.dma_start(raw[:, d % RAW, :].rearrange("p (c n) -> p c n", n=D),
                             w_out_chunks[:, c0:c0 + 2, :]).then_inc(raw_in[d % RAW], 16)
            with sp.Fori(0, ND // RAW) as i:
                for s in range(RAW):
                    sp.wait_ge(split_lo, i * RAW + (D_UP + s - RAW + 1))
                    sp.dma_start(raw[:, s, :].rearrange("p (c n) -> p c n", n=2 * P),
                                 w_up_chunks[:, :, ds(i * (RAW * 2 * P) + s * 2 * P, 2 * P)]).then_inc(raw_in[s], 16)
            with sp.Fori(0, ND // RAW) as i:
                for s in range(RAW):
                    sp.wait_ge(split_lo, i * RAW + (D_UP + ND + s - RAW + 1))
                    sp.dma_start(raw[:, s, :].rearrange("p (c n) -> p c n", n=D),
                                 w_down_chunks[:, ds(i * (2 * RAW) + 2 * s, 2), :]).then_inc(raw_in[s], 16)
            for t in range(NT):
                for h in range(2):
                    cols = slice(h * HALF, (h + 1) * HALF)
                    sp.wait_ge(y_ready, 2 * t + h + 1)
                    sp.dma_start(out[0, t * P:(t + 1) * P, cols], y_out[t % 2][:, cols]).then_inc(y_stored[t], 16)
            for t in range(NT):
                sp.wait_ge(y_stored[t], 32)

        @block.gpsimd
        def _(pool):
            steps = [0]
            used = [0]

            def link(ins):
                steps[0] += 1
                ins.then_inc(pool_step, 1)
                pool.wait_ge(pool_step, steps[0])

            def diagonal(tile, base, step):
                link(nc.gpsimd.memset(tile[:], 0.0))
                link(nc.gpsimd.affine_select(out=tile[:], in_=tile[:], compare_op=ALU.not_equal, fill=1.0, base=base,
                                             pattern=[[step, P]], channel_multiplier=1))

            diagonal(ident, 0, -1)
            diagonal(reverse, -(P - 1), 1)
            link(nc.gpsimd.memset(rel_tab[BUCKETS:BUCKETS + 1, :], MASKED))
            link(nc.gpsimd.memset(zero16[:], 0.0))
            link(nc.gpsimd.memset(ones[:], 1.0))
            link(nc.gpsimd.memset(nhalf[:], -0.5))
            pool.sem_inc(pool_const, 1)

            def rsqrt(dst, src, n, scale, eps):
                v = shifted[:, used[0]:used[0] + n]
                used[0] += n
                link(nc.gpsimd.tensor_scalar(v, src, scale, eps, ALU.mult, ALU.add))
                return nc.gpsimd.tensor_tensor(dst, v, nhalf[:, 0:n], ALU.pow)

            for t in range(NT):
                pool.wait_ge(x_squared, t + 1)
                rsqrt(r_x[:, t:t + 1], ss_x[:, t:t + 1], 1, 1.0 / D, EPS).then_inc(rx_ready, 1)

            pool.wait_ge(diag_copied, 1)
            pool.dma_start(rows_dram, diag_row).then_inc(rows_out, 16)
            pool.wait_ge(rows_out, 16)
            pool.dma_start(windows.rearrange("p (h n) -> p h n", n=NEAR),
                           bass.AP(rows_dram.tensor, 0, [[1, P], [SPAN, 8], [1, NEAR]])).then_inc(bias_in, 16)

            for n in range(NG):
                g = U_ORDER[n]
                w = WINDOWS[g]
                pool.wait_ge(u_copied, n + 1)
                if n == 0:
                    nc.gpsimd.memset(win_a[:, 0:PAD], 0.0)
                    link(nc.gpsimd.memset(win_b[:, 0:PAD], 0.0))
                    pool.wait_ge(const_in, 16 * 7)
                    pool.wait_ge(pad_ready, 1)
                else:
                    pool.wait_ge(mixed_ready, n)
                src, step = u_pad, 1
                dst, other = (win_a, win_b) if g % 2 == 0 else (win_b, win_a)
                while step < w:
                    link(nc.gpsimd.tensor_tensor(dst[:, PAD:], src[:, PAD:], src[:, PAD - step:PAD + SEQ - step],
                                                 ALU.add))
                    src, dst, other, step = dst, other, dst, 2 * step
                nc.gpsimd.tensor_tensor(src[:, PAD:2 * PAD], src[:, PAD:2 * PAD], edges[:, g * PAD:(g + 1) * PAD],
                                        ALU.mult).then_inc(window_ready, 1)

            pool.wait_ge(pool_ss, 1)
            rsqrt(r_pool, ss_pool_sb, NT, WS * WS / POOL_W, WS * WS * EPS).then_inc(rp_ready, 1)
            pool.wait_ge(attn_ss, 1)
            rsqrt(r_attn, ss_attn_sum, NT, WS * WS / POOL_W, WS * WS * EPS).then_inc(ra_ready, 1)
            for t in range(NT):
                pool.wait_ge(mix_squared, t + 1)
                rsqrt(r_mix[:, t:t + 1], ss_mix[:, t:t + 1], 1, 1.0 / D, EPS).then_inc(rm_ready, 1)
                pool.wait_ge(x1_squared, t + 1)
                rsqrt(r_x1[:, t:t + 1], ss_x1[:, t:t + 1], 1, 1.0 / D, EPS).then_inc(r1_ready, 1)
            for t in range(NT):
                pool.wait_ge(ff_squared, 2 * (t + 1))
                link(nc.gpsimd.tensor_tensor(ss_ff_sum[:, t:t + 1], ss_ff[:, 2 * t:2 * t + 1],
                                             ss_ff[:, 2 * t + 1:2 * t + 2], ALU.add))
                rsqrt(r_ff[:, t:t + 1], ss_ff_sum[:, t:t + 1], 1, 1.0 / D, WS * WS * EPS).then_inc(rf_ready, 1)

        def split_dst(d, part):
            if d < D_WO:
                return big[:, 2 * d:2 * d + 2, part, :]
            if d < D_UP:
                return wo[:, 2 * (d - D_WO):2 * (d - D_WO) + 2, part, :]
            if d == D_UP + 2 * ND - 1:
                return wo[:, 0:2, part, :]
            r = 2 * (d % 2)
            return ring[:, r:r + 2, part, :]

        def raw_halves(d):
            return raw[:, d % RAW, :].rearrange("p (s n) -> p s n", s=2)

        def split_hi_op(act, d, i=0):
            act.wait_ge(raw_in[d % RAW], i * 16 + loads_until(d))
            nc.scalar.activation(split_dst(d, 0), raw_halves(d), ACT.Copy, scale=WS).then_inc(split_hi, 1)

        def split_lo_op(dve, d, i=0):
            dve.wait_ge(split_hi, i * RAW + (d + 1))
            nc.vector.scalar_tensor_tensor(out=split_dst(d, 1), in0=raw_halves(d), scalar=WS, in1=split_dst(d, 0),
                                           op0=ALU.mult, op1=ALU.subtract).then_inc(split_lo, 1)

        @block.scalar
        def _(act):
            act.dma_start(row_pre, bass.AP(g_mix_pre.tensor, g_mix_pre.offset, [[0, P], [1, D]])).then_inc(row_in, 16)
            act.dma_start(rel_tab[0:BUCKETS, :], rel_bias).then_inc(const_in, 16)
            act.dma_start(onehot, bucket_rows).then_inc(const_in, 16)
            act.dma_start(vec_rows[0:NG, :], pool_scale.rearrange("a (g n) -> (a g) n", n=P)).then_inc(const_in, 16)
            act.dma_start(vec_rows[NG:2 * NG, :], g_pool_out.rearrange("a (g n) -> (a g) n", n=P)).then_inc(const_in, 16)
            act.dma_start(vec_rows[2 * NG:3 * NG, :], g_attn_out.rearrange("a (g n) -> (a g) n", n=P)).then_inc(const_in, 16)
            act.dma_start(wp_raw.rearrange("p (g n) -> p g n", g=NG), w_pool[0].rearrange("g c n -> c g n")).then_inc(const_in, 16)
            act.dma_start(edges[:], bass.AP(edge_table.tensor, edge_table.offset,
                                            [[0, P], [1, NG * PAD + NG]])).then_inc(const_in, 16)
            act.wait_ge(pool_const, 1)
            nc.scalar.activation(junk0[:, 0:1], ones[:], ACT.Square).then_inc(table_loaded, 1)
            act.wait_ge(table_loaded, 1)
            for t in range(NT):
                act.wait_ge(x_in[t], 16)
                if t >= 1:
                    act.wait_ge(x_squared, t)
                nc.scalar.activation(junk0, x_tok[:, t, :], ACT.Square,
                                     accum_out=ss_x[:, t:t + 1]).then_inc(x_squared, 1)

            def input_hi(chunks):
                for c in chunks:
                    act.wait_ge(xT_mm, c + 1)
                    nc.scalar.activation(hT[:, 0, c, :], bank[c][:], ACT.Copy).then_inc(hT_hi, 1)

            input_hi(range(0, 4))
            split_hi_op(act, 0)
            input_hi(range(4, KC))
            for d in range(1, D_WO):
                split_hi_op(act, d)
            act.wait_ge(const_in, 16 * 7)
            nc.scalar.activation(wp[:, 0, :, :].rearrange("p g n -> p (g n)"), wp_raw, ACT.Copy,
                                 scale=WS).then_inc(wp_hi, 1)
            for t in range(NT):
                act.wait_ge(v_mm, t + 1)
                nc.scalar.activation(v_hi[:, t, :], bank[t][:], ACT.Copy, scale=1 / WS).then_inc(v_hi_done, 1)
            for d in range(D_WO, D_UP):
                if d == D_WO + 1:
                    act.wait_ge(wp_lo, 1)
                    act.wait_ge(vec_ready, 3)
                    act.wait_ge(rows_out, 16)
                split_hi_op(act, d)
            for f in range(4):
                act.wait_ge(flip_mm, f + 1)
                nc.scalar.activation(bias[:, f * HALF:(f + 1) * HALF], O[f % 2][:], ACT.Copy).then_inc(bias_ready, 1)

            def qk_parts(p):
                act.wait_ge(qk_proj, 2 * p + 2)
                nc.scalar.activation(kT[:, 0, :], J[0][:], ACT.Copy, scale=1 / WS).then_inc(qk_hi, 1)
                nc.scalar.activation(qT[:, 0, :], J[1][:], ACT.Copy, scale=1 / WS / 8).then_inc(qk_hi, 1)

            def exp_step(p, s):
                n = (s % NT + 1) * P
                act.wait_ge(max_ready, p * STEPS + (s + 1))
                if s >= 2:
                    act.wait_ge(pT_mm, p * STEPS + (s - 1))
                c = s % 4
                nc.scalar.activation(prob[s % 2][:, 0:n], S[s % 2][:, 0:n], ACT.Exp, bias=neg_max[:, c:c + 1],
                                     accum_out=row_sum[:, c:c + 1]).then_inc(exp_done, 1)

            def pool_branch_hi(n):
                g = U_ORDER[n]
                act.wait_ge(pm_mm, n + 1)
                nc.scalar.activation(sq_pool[:, n * SEQ:(n + 1) * SEQ], J[n % 2][:], ACT.Square,
                                     scale=vecs[:, 3 * NG + g:3 * NG + g + 1]).then_inc(pm_sq, 1)
                nc.scalar.activation(y_half(SLOT_YP, g)[:, 0, :], J[n % 2][:], ACT.Copy,
                                     scale=vecs[:, 4 * NG + g:4 * NG + g + 1]).then_inc(pm_hi, 1)

            def pair(p, last):
                exp_step(p, 0)
                act.wait_ge(u_mm, p + 1)
                nc.scalar.activation(u_pad[:, PAD:], O[0][:], ACT.Copy, scale=1 / WS).then_inc(u_copied, 1)
                for s in range(STEPS):
                    if s + 1 < STEPS:
                        exp_step(p, s + 1)
                    n = (s % NT + 1) * P
                    act.wait_ge(pT_mm, p * STEPS + (s + 1))
                    if s >= 2:
                        act.wait_ge(pv_mm, p * STEPS + (s - 1))
                    nc.scalar.activation(pT[s % 2][:, 0, 0:n], PT[s % 2][:, 0:n], ACT.Copy).then_inc(pT_hi, 1)
                    if s == 5:
                        act.wait_ge(pooled, p + 1)
                        nc.scalar.activation(flat[:, ds((p * 3 + SLOT_U) * (2 * UNIT), SEQ)], win_a[:, PAD:],
                                             ACT.Copy).then_inc(mixed_hi, 1)
                    if last and s in (2, 3, 6):
                        pool_branch_hi((2, 3, 6).index(s))
                if not last:
                    act.wait_ge(score_mm, p * STEPS + STEPS)
                    qk_parts(p + 1)
                act.wait_ge(y_normed, p * STEPS + STEPS)
                for t in range(NT):
                    ins = nc.scalar.activation(junk1[:, t * P:(t + 1) * P], y_tok[:, t, :], ACT.Square,
                                               accum_out=ss_attn[:, ds(p * NT + t, 1)])
                ins.then_inc(y_squared, 1)
                act.wait_ge(yT_mm, p + 1)
                y_chunk = flat[:, ds(p * UNIT, SEQ)]
                nc.scalar.activation(y_chunk, PT[0][:], ACT.Copy,
                                     scale=vecs[:, ds(p + 2 * NG, 1)]).then_inc(yT_hi, 1)
                act.wait_ge(y_squared, p + 1)

            qk_parts(0)
            with act.Fori(0, NPAIR - 1) as p:
                pair(p, False)
            pair(NPAIR - 1, True)

            pool_branch_hi(NG - 1)
            act.wait_ge(mixed_ready, NG)
            for row, gain in ((row_mix_post, g_mix_post), (row_mlp_pre, g_mlp_pre), (row_mlp_post, g_mlp_post)):
                act.dma_start(row, bass.AP(gain.tensor, gain.offset, [[0, P], [1, D]])).then_inc(late_rows_in, 16)
            split_hi_op(act, D_UP)
            split_hi_op(act, D_UP + 1)

            def pool_share(t):
                for h in range(2):
                    act.wait_ge(outp_mm, 2 * t + h + 1)
                    nc.scalar.activation(mix(t)[:, h * HALF:(h + 1) * HALF], out_bank("pool", t, h)[:], ACT.Copy,
                                         scale=r_pool[:, t:t + 1]).then_inc(outp_scaled, 1)

            def mix_square(t):
                act.wait_ge(mix_ready, 2 * (t + 1))
                if t >= 1:
                    act.wait_ge(x1_squared, t)
                nc.scalar.activation(junk2, mix(t), ACT.Square, accum_out=ss_mix[:, t:t + 1]).then_inc(mix_squared, 1)

            def x1_square(t):
                act.wait_ge(x1_ready, t + 1)
                act.wait_ge(mix_squared, t + 1)
                nc.scalar.activation(junk2, x_tok[:, t, :], ACT.Square,
                                     accum_out=ss_x1[:, t:t + 1]).then_inc(x1_squared, 1)

            def input2_hi(t):
                for h in range(2):
                    act.wait_ge(x1T_mm, 2 * t + h + 1)
                    nc.scalar.activation(hT[:, 0, 4 * h:4 * h + 4, t * P:(t + 1) * P],
                                         J[h][:].rearrange("p (c n) -> p c n", n=P), ACT.Copy).then_inc(h2_hi, 1)

            act.wait_ge(rp_ready, 1)
            pool_share(0)
            pool_share(1)
            mix_square(0)
            x1_square(0)
            mix_square(1)
            x1_square(1)
            pool_share(2)
            input2_hi(0)
            input2_hi(1)
            mix_square(2)
            pool_share(3)
            x1_square(2)
            input2_hi(2)
            mix_square(3)
            x1_square(3)
            input2_hi(3)

            with act.Fori(0, ND // RAW) as i:
                for dd in range(RAW):
                    for e in range(2):
                        j = 2 * dd + e
                        act.wait_ge(up_mm, i * (2 * RAW) + (j + 1))
                        if j >= 2:
                            act.wait_ge(sq_done, i * (2 * RAW) + (j - 1))
                        nc.scalar.activation(relu[j % 2], bank[j % 4][:], ACT.Relu, scale=1 / WS).then_inc(relu_done, 1)
                        act.wait_ge(relu_done, i * (2 * RAW) + (j + 1))
                        nc.scalar.activation(flat[:, ds(i * (2 * RAW * UNIT) + j * UNIT, SEQ)], relu[j % 2],
                                             ACT.Square).then_inc(a_hi, 1)
                    split_hi_op(act, D_UP + 2 + dd, i)
                act.wait_ge(sq_done, i * (2 * RAW) + 2 * RAW)
            with act.Fori(0, ND // RAW - 1) as i:
                for dd in range(RAW):
                    act.wait_ge(down_mm, i * RAW + (dd + 1))
                    split_hi_op(act, D_UP + ND + 2 + dd, i)
            act.wait_ge(down_mm, ND - RAW + 1)
            split_hi_op(act, D_UP + 2 * ND - 2)
            split_hi_op(act, D_UP + 2 * ND - 1)
            for t in range(NT):
                for h in range(2):
                    act.wait_ge(ff_done, 2 * t + h + 1)
                    if 2 * t + h:
                        act.wait_ge(ff_squared, 2 * t + h)
                    nc.scalar.activation(junk2[:, 0:HALF], bank[2 * t + h][:], ACT.Square,
                                         accum_out=ss_ff[:, 2 * t + h:2 * t + h + 1]).then_inc(ff_squared, 1)

        @block.vector
        def _(dve):
            dve.sem_inc(yT_lo, 1)
            dve.wait_ge(row_in, 16)
            for t in range(NT):
                dve.wait_ge(rx_ready, t + 1)
                nc.vector.scalar_tensor_tensor(out=xs[t], in0=x_tok[:, t, :], scalar=r_x[:, t:t + 1], in1=row_pre,
                                               op0=ALU.mult, op1=ALU.mult).then_inc(xs_ready, 1)

            def input_lo(chunks):
                for c in chunks:
                    dve.wait_ge(hT_hi, c + 1)
                    nc.vector.tensor_tensor(hT[:, 1, c, :], bank[c][:], hT[:, 0, c, :], ALU.subtract).then_inc(hT_lo, 1)

            input_lo(range(0, 4))
            split_lo_op(dve, 0)
            input_lo(range(4, KC))
            split_lo_op(dve, 1)
            split_lo_op(dve, 2)
            dve.wait_ge(diag_mm, 1)
            nc.vector.tensor_copy(diag_row, bank[4][0:8, 0:SPAN]).then_inc(diag_copied, 1)
            dve.wait_ge(vec_mm, 1)
            nc.vector.tensor_copy(vecs[:, 0:3 * NG], bank[5][:, 0:3 * NG]).then_inc(vec_ready, 1)
            dve.wait_ge(vec_ready, 1)
            nc.vector.tensor_scalar(vecs[:, 3 * NG:4 * NG], vecs[:, 0:NG], 1 / WS, None, ALU.mult).then_inc(vec_ready, 1)
            dve.wait_ge(vec_ready, 2)
            nc.vector.tensor_tensor(vecs[:, 4 * NG:5 * NG], vecs[:, 3 * NG:4 * NG], vecs[:, NG:2 * NG],
                                    ALU.mult).then_inc(vec_ready, 1)
            nc.vector.memset(u_pad[:, 0:PAD], 0.0).then_inc(pad_ready, 1)
            for d in range(3, D_WO):
                split_lo_op(dve, d)
            dve.wait_ge(wp_hi, 1)
            nc.vector.scalar_tensor_tensor(out=wp[:, 1, :, :].rearrange("p g n -> p (g n)"), in0=wp_raw, scalar=WS,
                                           in1=wp[:, 0, :, :].rearrange("p g n -> p (g n)"), op0=ALU.mult,
                                           op1=ALU.subtract).then_inc(wp_lo, 1)
            for t in range(NT):
                dve.wait_ge(v_hi_done, t + 1)
                nc.vector.scalar_tensor_tensor(out=v_lo[:, t, :], in0=bank[t][:], scalar=1 / WS, in1=v_hi[:, t, :],
                                               op0=ALU.mult, op1=ALU.subtract).then_inc(v_lo_done, 1)
            for d in range(D_WO, D_UP):
                split_lo_op(dve, d)

            def qk_parts(p):
                dve.wait_ge(qk_hi, 2 * p + 1)
                nc.vector.scalar_tensor_tensor(out=kT[:, 1, :], in0=J[0][:], scalar=1 / WS, in1=kT[:, 0, :],
                                               op0=ALU.mult, op1=ALU.subtract).then_inc(qk_lo, 1)
                dve.wait_ge(qk_hi, 2 * p + 2)
                nc.vector.scalar_tensor_tensor(out=qT[:, 1, :], in0=J[1][:], scalar=1 / WS / 8, in1=qT[:, 0, :],
                                               op0=ALU.mult, op1=ALU.subtract).then_inc(qk_lo, 1)

            def max_step(p, s):
                i, h, b = s % NT, s // NT, s % 2
                n = (i + 1) * P
                near = min(NEAR, n)
                dve.wait_ge(score_mm, p * STEPS + (s + 1))
                nc.vector.tensor_tensor(S[b][:, n - near:n], S[b][:, n - near:n],
                                        bias[:, ds(p * (2 * NEAR) + (h * NEAR + NEAR - near), near)],
                                        ALU.add).then_inc(biased, 1)
                dve.wait_ge(biased, p * STEPS + (s + 1))
                c = s % 4
                nc.vector.tensor_reduce(neg_max[:, c:c + 1], S[b][:, 0:n], AX, ALU.max,
                                        negate=True).then_inc(max_ready, 1)

            def norm_step(p, s):
                i, h = s % NT, s // NT
                c = s % 4
                dve.wait_ge(pv_mm, p * STEPS + (s + 1))
                dve.wait_ge(inv_ready, p * STEPS + (s + 1))
                nc.vector.tensor_scalar(y_tok[:, i, h * HD:(h + 1) * HD], O[s % 2][:, 0:HD], row_inv[:, c:c + 1],
                                        None, ALU.mult).then_inc(y_normed, 1)

            def pool_branch_lo(n):
                g = U_ORDER[n]
                dve.wait_ge(pm_hi, n + 1)
                nc.vector.scalar_tensor_tensor(out=y_half(SLOT_YP, g)[:, 1, :], in0=J[n % 2][:],
                                               scalar=vecs[:, 4 * NG + g:4 * NG + g + 1],
                                               in1=y_half(SLOT_YP, g)[:, 0, :], op0=ALU.mult,
                                               op1=ALU.subtract).then_inc(pm_lo, 1)

            def pair(p, last):
                max_step(p, 0)
                for s in range(STEPS):
                    if s + 1 < STEPS:
                        max_step(p, s + 1)
                    n = (s % NT + 1) * P
                    c = s % 4
                    dve.wait_ge(exp_done, p * STEPS + (s + 1))
                    nc.vector.reciprocal(row_inv[:, c:c + 1], row_sum[:, c:c + 1]).then_inc(inv_ready, 1)
                    dve.wait_ge(pT_hi, p * STEPS + (s + 1))
                    nc.vector.tensor_tensor(pT[s % 2][:, 1, 0:n], PT[s % 2][:, 0:n], pT[s % 2][:, 0, 0:n],
                                            ALU.subtract).then_inc(pT_lo, 1)
                    if s >= 1:
                        norm_step(p, s - 1)
                    if s == 4:
                        dve.wait_ge(window_ready, p + 1)
                        nc.vector.scalar_tensor_tensor(out=win_a[:, PAD:], in0=win_a[:, PAD:],
                                                       scalar=edges[:, ds(p + NG * PAD, 1)], in1=u_pad[:, PAD:],
                                                       op0=ALU.mult, op1=ALU.subtract).then_inc(pooled, 1)
                    if s == 6:
                        dve.wait_ge(mixed_hi, p + 1)
                        place = (p * 3 + SLOT_U) * (2 * UNIT)
                        nc.vector.tensor_tensor(flat[:, ds(place + SEQ, SEQ)], win_a[:, PAD:],
                                                flat[:, ds(place, SEQ)], ALU.subtract).then_inc(mixed_ready, 1)
                    if last and s in (2, 3, 6):
                        pool_branch_lo((2, 3, 6).index(s))
                if not last:
                    qk_parts(p + 1)
                norm_step(p, STEPS - 1)
                dve.wait_ge(yT_hi, p + 1)
                dve.wait_ge(y_squared, p + 1)
                nc.vector.scalar_tensor_tensor(out=flat[:, ds(p * UNIT + SEQ, SEQ)], in0=PT[0][:],
                                               scalar=vecs[:, ds(p + 2 * NG, 1)], in1=flat[:, ds(p * UNIT, SEQ)],
                                               op0=ALU.mult, op1=ALU.subtract).then_inc(yT_lo, 1)

            qk_parts(0)
            dve.wait_ge(bias_ready, 4)
            with dve.Fori(0, NPAIR - 1) as p:
                pair(p, False)
            pair(NPAIR - 1, True)

            dve.wait_ge(y_squared, NPAIR)
            nc.vector.tensor_reduce(ss_attn_sum, ss_attn.rearrange("p (c t) -> p t c", c=NPAIR), AX,
                                    ALU.add).then_inc(attn_ss, 1)
            pool_branch_lo(NG - 1)
            split_lo_op(dve, D_UP)
            dve.wait_ge(pool_ss_mm, 1)
            nc.vector.tensor_copy(ss_pool_sb, J[0][:, 0:NT]).then_inc(pool_ss, 1)
            split_lo_op(dve, D_UP + 1)
            dve.wait_ge(ra_ready, 1)
            dve.wait_ge(late_rows_in, 16 * 3)

            def add_shares(t):
                for h in range(2):
                    dve.wait_ge(outa_mm, 2 * t + h + 1)
                    dve.wait_ge(outp_scaled, 2 * t + h + 1)
                    m = mix(t)[:, h * HALF:(h + 1) * HALF]
                    nc.vector.scalar_tensor_tensor(out=m, in0=out_bank("attn", t, h)[:], scalar=r_attn[:, t:t + 1],
                                                   in1=m, op0=ALU.mult, op1=ALU.add).then_inc(mix_ready, 1)

            def residual(t):
                dve.wait_ge(rm_ready, t + 1)
                nc.vector.scalar_tensor_tensor(out=mix(t), in0=mix(t), scalar=r_mix[:, t:t + 1], in1=row_mix_post,
                                               op0=ALU.mult, op1=ALU.mult).then_inc(mix_scaled, 1)
                dve.wait_ge(mix_scaled, t + 1)
                nc.vector.tensor_tensor(x_tok[:, t, :], x_tok[:, t, :], mix(t), ALU.add).then_inc(x1_ready, 1)

            def norm_x1(t):
                dve.wait_ge(r1_ready, t + 1)
                if t >= 2:
                    dve.wait_ge(x1T_mm, 2 * (t - 1))
                nc.vector.scalar_tensor_tensor(out=xs2[t % 2], in0=x_tok[:, t, :], scalar=r_x1[:, t:t + 1],
                                               in1=row_mlp_pre, op0=ALU.mult, op1=ALU.mult).then_inc(xs2_ready, 1)

            def input2_lo(t):
                for h in range(2):
                    dve.wait_ge(h2_hi, 2 * t + h + 1)
                    nc.vector.tensor_tensor(hT[:, 1, 4 * h:4 * h + 4, t * P:(t + 1) * P],
                                            J[h][:].rearrange("p (c n) -> p c n", n=P),
                                            hT[:, 0, 4 * h:4 * h + 4, t * P:(t + 1) * P],
                                            ALU.subtract).then_inc(h2_lo, 1)

            add_shares(0)
            residual(0)
            add_shares(1)
            norm_x1(0)
            residual(1)
            input2_lo(0)
            norm_x1(1)
            add_shares(2)
            input2_lo(1)
            residual(2)
            norm_x1(2)
            add_shares(3)
            input2_lo(2)
            residual(3)
            norm_x1(3)
            input2_lo(3)

            with dve.Fori(0, ND // RAW) as i:
                for dd in range(RAW):
                    for e in range(2):
                        j = 2 * dd + e
                        dve.wait_ge(relu_done, i * (2 * RAW) + (j + 1))
                        if j >= 2:
                            dve.wait_ge(a_lo, i * (2 * RAW) + (j - 1))
                        nc.vector.tensor_tensor(squared[j % 2], relu[j % 2], relu[j % 2], ALU.mult).then_inc(sq_done, 1)
                        dve.wait_ge(sq_done, i * (2 * RAW) + (j + 1))
                        dve.wait_ge(a_hi, i * (2 * RAW) + (j + 1))
                        nc.vector.tensor_tensor(flat[:, ds(i * (2 * RAW * UNIT) + (j * UNIT + SEQ), SEQ)],
                                                squared[j % 2],
                                                flat[:, ds(i * (2 * RAW * UNIT) + j * UNIT, SEQ)],
                                                ALU.subtract).then_inc(a_lo, 1)
                    split_lo_op(dve, D_UP + 2 + dd, i)
                dve.wait_ge(a_lo, i * (2 * RAW) + 2 * RAW)
            with dve.Fori(0, ND // RAW - 1) as i:
                for dd in range(RAW):
                    split_lo_op(dve, D_UP + ND + 2 + dd, i)
            for dd in range(2):
                split_lo_op(dve, D_UP + 2 * ND - 2 + dd)

            for t in range(NT):
                dve.wait_ge(rf_ready, t + 1)
                if t >= 2:
                    dve.wait_ge(y_stored[t - 2], 32)
                for h in range(2):
                    cols = slice(h * HALF, (h + 1) * HALF)
                    nc.vector.scalar_tensor_tensor(out=y_out[t % 2][:, cols], in0=bank[2 * t + h][:],
                                                   scalar=r_ff[:, t:t + 1], in1=row_mlp_post[:, cols], op0=ALU.mult,
                                                   op1=ALU.mult).then_inc(ff_scaled, 1)
                    dve.wait_ge(ff_scaled, 2 * t + h + 1)
                    nc.vector.tensor_tensor(y_out[t % 2][:, cols], y_out[t % 2][:, cols], x_tok[:, t, cols],
                                            ALU.add).then_inc(y_ready, 1)

        @block.tensor
        def _(pe):
            def passes(dst, w_hi, w_lo, m_hi, m_lo, first, final):
                nc.tensor.matmul(dst, w_hi, m_hi, start=first, stop=False)
                nc.tensor.matmul(dst, w_hi, m_lo, start=False, stop=False)
                return nc.tensor.matmul(dst, w_lo, m_hi, start=False, stop=final)

            pe.wait_ge(pool_const, 1)
            for t in range(NT):
                pe.wait_ge(xs_ready, t + 1)
                for c in range(KC):
                    ins = nc.tensor.transpose(bank[c][:, t * P:(t + 1) * P], xs[t][:, c * P:(c + 1) * P], ident[:])
                    if t == NT - 1:
                        ins.then_inc(xT_mm, 1)
            for c in range(KC):
                pe.wait_ge(hT_lo, max(c + 1, NT))
                if c % 4 == 0:
                    pe.wait_ge(split_lo, c // 4 + 1)
                w = big[:, SLOT_V + c // 2, :, (c % 2) * HALF:(c % 2) * HALF + HALF]
                for t in range(NT):
                    ins = passes(bank[t][:], hT[:, 0, c, t * P:(t + 1) * P], hT[:, 1, c, t * P:(t + 1) * P],
                                 w[:, 0, :], w[:, 1, :], c == 0, c == KC - 1)
                    if c == KC - 1:
                        ins.then_inc(v_mm, 1)
                if c == 4:
                    pe.wait_ge(hT_lo, 6)
                    pe.wait_ge(const_in, 16 * 7)
                    nc.tensor.matmul(bank[4][0:8, 0:SPAN], rel_tab, onehot, start=True, stop=True).then_inc(diag_mm, 1)
                    nc.tensor.transpose(bank[5][:, 0:3 * NG], vec_rows, ident[0:3 * NG, 0:3 * NG]).then_inc(vec_mm, 1)

            def project(dst, slot, chunks):
                for c in chunks:
                    ins = passes(dst, flat[:, ds(slot * (2 * UNIT) + c * P, P)],
                                 flat[:, ds(slot * (2 * UNIT) + (UNIT + c * P), P)],
                                 hT[:, 0, c, :], hT[:, 1, c, :], c == 0, c == KC - 1)
                return ins

            def scores(p, s):
                i, h, b = s % NT, s // NT, s % 2
                n = (i + 1) * P
                if s >= 2:
                    pe.wait_ge(exp_done, p * STEPS + (s - 1))
                rows = slice(h * HD, (h + 1) * HD)
                passes(S[b][:, 0:n], qT[rows, 0, i * P:(i + 1) * P], qT[rows, 1, i * P:(i + 1) * P],
                       kT[rows, 0, 0:n], kT[rows, 1, 0:n], True, True).then_inc(score_mm, 1)

            def transpose_probs(p, s):
                pe.wait_ge(exp_done, p * STEPS + (s + 1))
                if s == 0:
                    pe.wait_ge(yT_lo, p + 1)
                for j in range(s % NT + 1):
                    ins = nc.tensor.transpose(PT[s % 2][:, j * P:(j + 1) * P], prob[s % 2][:, j * P:(j + 1) * P],
                                              ident[:])
                ins.then_inc(pT_mm, 1)

            def outputs(p, s):
                i, h, b = s % NT, s // NT, s % 2
                pe.wait_ge(pT_lo, p * STEPS + (s + 1))
                if s >= 2:
                    pe.wait_ge(y_normed, p * STEPS + (s - 1))
                for j in range(i + 1):
                    cols = ds(p * P + h * HD, HD)
                    ins = passes(O[b][:, 0:HD], pT[b][:, 0, j * P:(j + 1) * P], pT[b][:, 1, j * P:(j + 1) * P],
                                 v_hi[:, j, cols], v_lo[:, j, cols], j == 0, j == i)
                ins.then_inc(pv_mm, 1)

            def fill(p, s):
                if s < 6:
                    chunks = (range(0, 3), range(3, 6), range(6, 8))[s % 3]
                    if s < 3:
                        ins = project(J[1][:], p * 3 + (SLOT_Q + 3), chunks)
                    else:
                        ins = project(J[0][:], p * 3 + (SLOT_K + 3), chunks)
                    if s % 3 == 2:
                        ins.then_inc(qk_proj, 1)

            def pool_product(n):
                g = U_ORDER[n]
                pe.wait_ge(mixed_ready, n + 1)
                if n >= 2:
                    pe.wait_ge(pm_lo, n - 1)
                    pe.wait_ge(pm_sq, n - 1)
                passes(J[n % 2][:], wp[:, 0, g, :], wp[:, 1, g, :], mixed[n][:, 0, :], mixed[n][:, 1, :], True,
                       True).then_inc(pm_mm, 1)

            def pair(p, last):
                pe.wait_ge(qk_lo, p * 2 + 2)
                scores(p, 0)
                scores(p, 1)
                project(O[0][:], p * 3 + SLOT_U, range(4, 8)).then_inc(u_mm, 1)
                transpose_probs(p, 0)
                for s in range(STEPS):
                    if s + 2 < STEPS:
                        scores(p, s + 2)
                    if s + 1 < STEPS:
                        transpose_probs(p, s + 1)
                    if not last:
                        fill(p, s)
                    elif s in (0, 1, 4):
                        pool_product((0, 1, 4).index(s))
                    if s == 0:
                        pe.wait_ge(u_copied, p + 1)
                    outputs(p, s)
                if not last:
                    pe.wait_ge(y_normed, p * STEPS + (STEPS - 1))
                    project(O[0][:], p * 3 + (SLOT_U + 3), range(0, 4))
                else:
                    pool_product(NG - 1)
                pe.wait_ge(y_normed, p * STEPS + STEPS)
                for t in range(NT):
                    ins = nc.tensor.transpose(PT[0][:, t * P:(t + 1) * P], y_tok[:, t, :], ident[:])
                ins.then_inc(yT_mm, 1)

            pe.wait_ge(split_lo, 3)
            pe.wait_ge(hT_lo, KC)
            project(J[1][:], SLOT_Q, range(KC)).then_inc(qk_proj, 1)
            project(J[0][:], SLOT_K, range(KC)).then_inc(qk_proj, 1)
            pe.wait_ge(bias_in, 16)
            pe.wait_ge(vec_ready, 1)
            for f in range(4):
                if f >= 2:
                    pe.wait_ge(bias_ready, f - 1)
                nc.tensor.matmul(O[f % 2][:], reverse[:], windows[:, f * HALF:(f + 1) * HALF], start=True,
                                 stop=True).then_inc(flip_mm, 1)
            pe.wait_ge(split_lo, D_WO)
            pe.wait_ge(bias_ready, 3)
            project(O[0][:], SLOT_U, range(0, 4))
            pe.wait_ge(bias_ready, 4)
            pe.wait_ge(v_lo_done, NT)
            with pe.Fori(0, NPAIR - 1) as p:
                pair(p, False)
            pair(NPAIR - 1, True)

            def out_project(br, t, h):
                dst, slot, first_chunk = out_bank(br, t, h), SLOT_YP, 0
                if br == "attn":
                    slot, first_chunk = SLOT_YA, NG
                i = out_groups.index((br, t, h))
                if i >= 6:
                    before, t0, h0 = out_groups[i - 6]
                    pe.wait_ge(outp_scaled if before == "pool" else mix_ready, 2 * t0 + h0 + 1)
                for n, c in enumerate(U_ORDER):
                    if i == 0 and n == NG - 1:
                        pe.wait_ge(pm_lo, NG)
                    y = y_half(slot, c)
                    w = wo[:, first_chunk + c, :, h * HALF:(h + 1) * HALF]
                    ins = passes(dst[:], y[:, 0, t * P:(t + 1) * P], y[:, 1, t * P:(t + 1) * P], w[:, 0, :], w[:, 1, :],
                                 n == 0, n == NG - 1)
                ins.then_inc(outp_mm if br == "pool" else outa_mm, 1)

            def transpose_x1(t):
                pe.wait_ge(xs2_ready, t + 1)
                for h in range(2):
                    if t >= 1:
                        pe.wait_ge(h2_lo, 2 * (t - 1) + h + 1)
                    for c in range(4):
                        ins = nc.tensor.transpose(J[h][:, c * P:(c + 1) * P],
                                                  xs2[t % 2][:, (4 * h + c) * P:(4 * h + c + 1) * P], ident[:])
                    ins.then_inc(x1T_mm, 1)

            pe.wait_ge(split_lo, D_UP)
            pe.wait_ge(pm_lo, NG - 1)
            for br, t, h in out_groups:
                if (br, t, h) == ("pool", 1, 0):
                    pe.wait_ge(pm_sq, NG)
                    for tt in range(NT):
                        for n in range(NG):
                            ins = nc.tensor.matmul(J[0][:, tt:tt + 1],
                                                   sq_pool[:, n * SEQ + tt * P:n * SEQ + (tt + 1) * P], ones[:],
                                                   start=(n == 0), stop=(n == NG - 1))
                    ins.then_inc(pool_ss_mm, 1)
                if (br, t, h) == ("attn", 0, 0):
                    pe.wait_ge(yT_lo, NPAIR + 1)
                if (br, t, h) == ("attn", 2, 0):
                    pe.wait_ge(pool_ss, 1)
                    transpose_x1(0)
                if (br, t, h) == ("pool", 3, 0):
                    transpose_x1(1)
                out_project(br, t, h)
            transpose_x1(2)

            def up(j, e, r, cols=slice(0, SEQ)):
                for c in range(KC):
                    w = slice((c % 4) * 2 * P + e * P, (c % 4) * 2 * P + (e + 1) * P)
                    ins = passes(bank[j][:, cols], ring[:, r + c // 4, 0, w], ring[:, r + c // 4, 1, w],
                                 hT[:, 0, c, cols], hT[:, 1, c, cols], c == 0, c == KC - 1)
                return ins

            pe.wait_ge(split_lo, D_UP + 1)
            pe.wait_ge(h2_lo, 2 * (NT - 1))
            pe.wait_ge(outp_scaled, 2 * NT)
            for e in range(2):
                up(e, e, 0, slice(0, SEQ - P))
            transpose_x1(NT - 1)
            pe.wait_ge(h2_lo, 2 * NT)
            for e in range(2):
                up(e, e, 0, slice(SEQ - P, SEQ)).then_inc(up_mm, 1)
            pe.wait_ge(split_lo, D_UP + 2)
            for e in range(2):
                up(2 + e, e, 2).then_inc(up_mm, 1)
            with pe.Fori(1, ND // 2) as i:
                for dd in range(2):
                    pe.wait_ge(split_lo, i * 2 + (D_UP + dd + 1))
                    for e in range(2):
                        up(2 * dd + e, e, 2 * dd).then_inc(up_mm, 1)

            pe.wait_ge(relu_done, NF)
            for b in range(2 * NT):
                nc.tensor.matmul(bank[b][:, 0:1], zero16[:], zero16[:, 0:1], start=True, stop=False,
                                 skip_group_check=True)

            def down(j, w, tiles, halves=(0, 1)):
                for t in tiles:
                    for h in halves:
                        for part_a, part_w in ((0, 0), (0, 1), (1, 0)):
                            ins = nc.tensor.matmul(bank[2 * t + h][:],
                                                   flat[:, ds(j * UNIT + (part_a * SEQ + t * P), P)],
                                                   w[:, part_w, h * HALF:(h + 1) * HALF], start=False,
                                                   stop=False, skip_group_check=True)
                return ins

            with pe.Fori(0, ND // RAW - 1) as i:
                for dd in range(RAW):
                    pe.wait_ge(split_lo, i * RAW + (D_UP + ND + dd + 1))
                    pe.wait_ge(a_lo, i * (2 * RAW) + (2 * dd + 2))
                    for e in range(2):
                        ins = down(i * (2 * RAW) + (2 * dd + e), ring[:, 2 * (dd % 2) + e], range(NT))
                    ins.then_inc(down_mm, 1)
            pe.wait_ge(a_lo, NF)
            for dd in range(2):
                pe.wait_ge(split_lo, D_UP + 2 * ND - RAW + dd + 1)
                for e in range(2):
                    ins = down(NF - 2 * RAW + 2 * dd + e, ring[:, 2 * dd + e], range(NT))
                ins.then_inc(down_mm, 1)
            pe.wait_ge(split_lo, D_UP + 2 * ND)
            for t in range(NT):
                for h in range(2):
                    for e in range(4):
                        ins = down(NF - 4 + e, ring[:, e] if e < 2 else wo[:, e - 2], [t], [h])
                    ins.then_inc(ff_done, 1)


_INS = ['x', 'w_in', 'w_pool', 'pool_scale', 'rel_bias', 'g_mix_pre', 'g_pool_out', 'g_attn_out', 'w_out',
        'g_mix_post', 'g_mlp_pre', 'w_up', 'w_down', 'g_mlp_post']


def _shape_constants():
    import math as _math
    import numpy as _np
    dist = NEAR - 1 - _np.arange(SPAN)
    exact = BUCKETS // 2
    far = _np.log(_np.maximum(dist, exact).astype(_np.float32) / _np.float32(exact)) / _np.float32(_math.log(8.0))
    bucket = _np.where(dist < exact, _np.maximum(dist, 0),
                       _np.minimum(exact + (far * _np.float32(BUCKETS - exact)).astype(_np.int32), BUCKETS - 1))
    rows = _np.zeros((BUCKETS + 1, SPAN), _np.float32)
    rows[bucket, _np.arange(SPAN)] = 1.0
    rows[BUCKETS - 1] -= 1.0
    rows[BUCKETS] = dist < 0
    edges = [w / min(t + 1, w) for w in WINDOWS for t in range(PAD)] + [1 / WINDOWS[g] for g in U_ORDER]
    return rows, _np.array([edges], _np.float32)


def kernel(**inputs):
    import numpy as _np
    import concourse.bacc as _bacc
    from concourse import mybir as _mybir
    from concourse.bass_utils import run_bass_kernel_spmd as _run

    nc = _bacc.Bacc("TRN2", target_bir_lowering=False, num_devices=1)
    rows, edges = _shape_constants()
    arrays, args = {}, []
    for name, a in [(n, inputs[n]) for n in _INS] + [("bucket_rows", rows), ("edge_table", edges)]:
        a = _np.ascontiguousarray(a)
        arrays[f"in_{name}_dram"] = a
        args.append(nc.dram_tensor(f"in_{name}_dram", a.shape, _mybir.dt.from_np(a.dtype), kind="ExternalInput").ap())
    args.append(nc.dram_tensor("out_0_dram", (1, SEQ, D), _mybir.dt.float32, kind="ExternalOutput").ap())
    hybrid_layer(nc, *args)
    r = _run(nc, [arrays], core_ids=[0])
    return r.results[0]["out_0_dram"]
```

```python
from contextlib import ExitStack

import concourse.bass as bass
from concourse import mybir

F32 = mybir.dt.float32
F16 = mybir.dt.float16
ALU = mybir.AluOpType
ACT = mybir.ActivationFunctionType
AX = mybir.AxisListType.X
ds = bass.ds

P = 128
SEQ, D = 512, 1024
NT = SEQ // P
KC = D // P
HALF = 512
POOL_W = D // 2
WINDOWS = (2, 4, 8, 16)
NG = len(WINDOWS)
PAD = max(WINDOWS)
HD = 64
NPAIR = POOL_W // P
STEPS = 2 * NT
D_FF = 4 * D
NF = D_FF // P
BUCKETS = 32
NEAR = 2 * P
SPAN = 3 * P
WS = 32.0
EPS = 1e-6
MASKED = -1e30
UNIT = 1024
RAW = 4

SLOT_V = 0
SLOT_Q, SLOT_K, SLOT_U = 4, 5, 6
U_ORDER = (3, 0, 1, 2)
SLOT_YA, SLOT_YP = 0, 4
SLOT_SQ = 2
SLOT_MIX = (7, 8, 10, 11)
D_WO, D_UP = 8, 12
ND = NF // 2


def loads_until(d):
    return sum(32 if 2 <= e < D_WO else 16 for e in range(d % RAW, d + 1, RAW))


def hybrid_layer(nc, x, w_in, w_pool, pool_scale, rel_bias, g_mix_pre, g_pool_out, g_attn_out,
                 w_out, g_mix_post, g_mlp_pre, w_up, w_down, g_mlp_post, bucket_rows, edge_table, out):
    ctx = ExitStack()
    with ctx:
        def sb(name, shape, dt=F32):
            return ctx.enter_context(nc.sbuf_tensor(name, shape, dt))

        def sem(name):
            return ctx.enter_context(nc.semaphore(name))

        x_tok = sb("x_tok", [P, NT, D])
        hT = sb("hT", [P, 2, KC, SEQ], F16)
        raw = sb("raw", [P, RAW, 2 * UNIT])
        big = sb("big", [P, 16, 2, UNIT], F16)
        wo = sb("wo", [P, KC, 2, UNIT], F16)
        ring = sb("ring", [P, 4, 2, UNIT], F16)
        scr = sb("scr", [P, 6144])
        ident = sb("ident", [P, P])
        reverse = sb("reverse", [P, P])
        ones = sb("ones", [P, 1])
        nhalf = sb("nhalf", [P, 2 * NT])
        edges = sb("edges", [P, NG * PAD + NG])
        wp = sb("wp", [P, 2 * NG * P], F16)
        vecs = sb("vecs", [P, 5 * NG + KC])
        zero16 = sb("zero16", [P, P], F16)
        stat = sb("stat", [P, 112])

        flat = big[:, :, :, :].rearrange("p s a n -> p (s a n)")
        raw_flat, wo_flat = raw[:, :, :].rearrange("p r n -> p (r n)"), wo[:, :, :, :].rearrange("p s a n -> p (s a n)")
        v_hi = ring[:, 0, :, :].rearrange("p a (t n) -> p (a t) n", n=HALF)
        v_lo = ring[:, 1, :, :].rearrange("p a (t n) -> p (a t) n", n=HALF)
        bias = ring[:, 2:4, :, :].rearrange("p s a n -> p (s a n)").bitcast(F32)
        late = wo[:, 6:8, :, :].rearrange("p s a n -> p (s a n)").bitcast(F32)
        onehot, diag_row, wp_raw = late[0:BUCKETS + 1, 0:SPAN], late[0:8, 384:384 + SPAN], late[:, 1024:1536]
        vec_rows, rel_tab, pre_rows = late[0:3 * NG, 768:896], late[0:BUCKETS + 1, 896:904], late[0:KC, 1536:1664]

        def by_tile(row):
            return row.rearrange("p (t n) -> p t n", n=P)

        def mix(t):
            return big[:, SLOT_MIX[t], :, :].rearrange("p a n -> p (a n)").bitcast(F32)

        def y_half(slot, c):
            return big[:, slot + c // 2, c % 2, :].rearrange("p (a n) -> p a n", a=2)

        sq_pool = big[:, SLOT_SQ:SLOT_SQ + 2, :, :].rearrange("p s a n -> p (s a n)").bitcast(F32)

        xs = [scr[:, UNIT * t:UNIT * (t + 1)] for t in range(NT)]
        junk0 = scr[:, 5120:6144]
        prob = [scr[:, 0:512], scr[:, 512:1024]]
        pT = [scr[:, 1024 + 512 * b:1536 + 512 * b].bitcast(F16).rearrange("p (a n) -> p a n", a=2) for b in range(2)]
        qT = scr[:, 2048:2560].bitcast(F16).rearrange("p (a n) -> p a n", a=2)
        kT = scr[:, 2560:3072].bitcast(F16).rearrange("p (a n) -> p a n", a=2)
        u_pad, win_a, win_b = (scr[:, 3072 + 528 * n:3600 + 528 * n] for n in range(3))
        y_tok = scr[:, 4656:5168].rearrange("p (t n) -> p t n", t=NT)
        junk1 = scr[:, 5168:5680]
        xs2 = [scr[:, 0:1024], scr[:, 1024:2048]]
        row_mix_post, row_mlp_pre, junk2, row_mlp_post = (scr[:, 2048 + 1024 * n:3072 + 1024 * n] for n in range(4))
        relu = [scr[:, 0:512], scr[:, 512:1024]]
        squared = [scr[:, 1024:1536], scr[:, 1536:2048]]
        y_out = [scr[:, 0:1024], scr[:, 1024:2048]]

        ss_x, r_x = stat[:, 0:4], stat[:, 4:8]
        neg_max, row_sum, row_inv = stat[:, 8:12], stat[:, 12:16], stat[:, 16:20]
        ss_attn = stat[:, 20:36]
        r_branches, r_pool, r_attn = stat[:, 36:44], stat[:, 36:40], stat[:, 40:44]
        ss_mix, r_mix, ss_x1, r_x1 = stat[:, 44:48], stat[:, 48:52], stat[:, 52:56], stat[:, 56:60]
        ss_ff, r_ff = stat[:, 60:68], stat[:, 68:72]
        ss_branches, half_ff = stat[:, 72:80], stat[:, 80:84]
        ss_attn_sum = stat[:, 84:88]
        shifted = stat[:, 88:112]

        bank = [ctx.enter_context(nc.psum_tensor(f"bank{i}", [P, HALF], F32)) for i in range(8)]
        S, PT, O, J = bank[0:2], bank[2:4], bank[4:6], bank[6:8]

        q_psum = J[1][:]
        q_reversed = bass.AP(q_psum.tensor, q_psum.offset + P - 1, [list(q_psum.ap[0]), [P, NT], [-1, P]])

        rows_dram = nc.dram_tensor("diag_rows_dram", (8, SPAN), F32, kind="Internal").ap()

        x_in = [sem(f"x_in{t}") for t in range(NT)]
        raw_in = [sem(f"raw_in{s}") for s in range(RAW)]
        const_in, pre_in, rows_out, bias_in, late_rows_in = (
            sem(n) for n in ("const_in", "pre_in", "rows_out", "bias_in", "late_rows_in"))
        y_stored = [sem(f"y_stored{t}") for t in range(NT)]
        pool_const, pool_step = sem("pool_const"), sem("pool_step")
        x_squared, rx_ready, xs_ready, xT_mm, hT_hi, hT_lo = (
            sem(n) for n in ("x_squared", "rx_ready", "xs_ready", "xT_mm", "hT_hi", "hT_lo"))
        vec_mm, vec_ready, diag_mm, diag_copied, wp_hi, wp_lo = (
            sem(n) for n in ("vec_mm", "vec_ready", "diag_mm", "diag_copied", "wp_hi", "wp_lo"))
        gain_mm, gain_ready = sem("gain_mm"), sem("gain_ready")
        split_hi, split_lo = sem("split_hi"), sem("split_lo")
        first_hi, first_lo = sem("first_hi"), sem("first_lo")
        v_mm, v_hi_done, v_lo_done = sem("v_mm"), sem("v_hi_done"), sem("v_lo_done")
        qk_proj, qk_hi, qk_lo, u_mm, u_copied, window_ready, pooled, mixed_hi, mixed_ready = (
            sem(n) for n in ("qk_proj", "qk_hi", "qk_lo", "u_mm", "u_copied", "window_ready", "pooled", "mixed_hi",
                             "mixed_ready"))
        table_loaded, pad_ready = sem("table_loaded"), sem("pad_ready")
        score_mm, biased, max_ready, exp_done, pT_mm, pT_hi, pT_lo, inv_ready, pv_mm, y_normed = (
            sem(n) for n in ("score_mm", "biased", "max_ready", "exp_done", "pT_mm", "pT_hi", "pT_lo",
                             "inv_ready", "pv_mm", "y_normed"))
        y_squared, yT_mm, yT_hi, yT_lo = (sem(n) for n in ("y_squared", "yT_mm", "yT_hi", "yT_lo"))
        pm_mm, pm_sq, pm_hi, pm_lo, branch_ss_mm, branch_ss, attn_ss = (
            sem(n) for n in ("pm_mm", "pm_sq", "pm_hi", "pm_lo", "branch_ss_mm", "branch_ss", "attn_ss"))
        squares_ready = sem("squares_ready")
        branch_r_ready, outp_mm, outp_scaled, outa_mm, mix_ready = (
            sem(n) for n in ("branch_r_ready", "outp_mm", "outp_scaled", "outa_mm", "mix_ready"))
        mix_squared, rm_ready, mix_scaled, x1_ready, x1_squared, r1_ready, xs2_ready = (
            sem(n) for n in ("mix_squared", "rm_ready", "mix_scaled", "x1_ready", "x1_squared", "r1_ready",
                             "xs2_ready"))
        x1T_mm, h2_hi, h2_lo = sem("x1T_mm"), sem("h2_hi"), sem("h2_lo")
        up_mm, relu_done, sq_done, a_hi, a_lo = (sem(n) for n in ("up_mm", "relu_done", "sq_done", "a_hi", "a_lo"))
        down_mm, ff_done, ff_squared, rf_ready, ff_scaled, y_ready = (
            sem(n) for n in ("down_mm", "ff_done", "ff_squared", "rf_ready", "ff_scaled", "y_ready"))

        out_groups = [(br, t, h) for br, t in (("pool", 0), ("pool", 1), ("attn", 0), ("attn", 1), ("pool", 2),
                                               ("attn", 2), ("pool", 3), ("attn", 3)) for h in range(2)]

        def out_bank(br, t, h):
            i = out_groups.index((br, t, h))
            return J[i] if i < 2 else bank[(4, 5, 2, 3, 0, 1)[(i - 2) % 6]]

        block = ctx.enter_context(nc.Block())

        @block.sync
        def _(sp):
            for t in range(NT):
                sp.dma_start(x_tok[:, t, :], x[0, t * P:(t + 1) * P, :]).then_inc(x_in[t], 16)

            w_in_chunks = w_in[0].rearrange("(c p) n -> p c n", p=P)
            w_out_chunks = w_out[0].rearrange("(c p) n -> p c n", p=P)
            w_up_chunks = w_up[0].rearrange("(c p) n -> p c n", p=P)
            w_down_chunks = w_down[0].rearrange("(c p) n -> p c n", p=P)

            scale_rows = pool_scale.rearrange("a (g n) -> (a g) n", n=P)
            gain_rows = g_pool_out.rearrange("a (g n) -> (a g) n", n=P)

            def wait_raw_free(d):
                if d >= RAW:
                    sp.wait_ge(split_lo, d - RAW + 1)

            for d in range(2):
                sp.dma_start(raw[:, d, :].rearrange("p (c n) -> p c n", n=HALF),
                             w_in_chunks[:, 4 * d:4 * d + 4, 3 * POOL_W:4 * POOL_W]).then_inc(raw_in[d], 16)
            columns = []
            for n in range(NPAIR):
                columns += [POOL_W + n * P, 2 * POOL_W + n * P, U_ORDER[n] * P]
            for d in range(2, D_WO):
                if d == RAW:
                    for dst, src in ((rel_tab[0:BUCKETS, :], rel_bias),
                                     (onehot, bucket_rows),
                                     (vec_rows[0:1, :], scale_rows[NG - 1:NG, :]),
                                     (vec_rows[1:NG, :], scale_rows[0:NG - 1, :]),
                                     (vec_rows[NG:NG + 1, :], gain_rows[NG - 1:NG, :]),
                                     (vec_rows[NG + 1:2 * NG, :], gain_rows[0:NG - 1, :]),
                                     (vec_rows[2 * NG:3 * NG, :], g_attn_out.rearrange("a (g n) -> (a g) n", n=P)),
                                     (wp_raw[:, 0:P], w_pool[0, NG - 1]),
                                     (wp_raw[:, P:NG * P].rearrange("p (g n) -> p g n", n=P),
                                      w_pool[0, 0:NG - 1].rearrange("g c n -> c g n")),
                                     (edges[:], bass.AP(edge_table.tensor, edge_table.offset,
                                                        [[0, P], [1, NG * PAD + NG]]))):
                        sp.dma_start(dst, src).then_inc(const_in, 16)
                wait_raw_free(d)
                for e in range(2):
                    c0 = columns[2 * (d - 2) + e]
                    sp.dma_start(raw[:, d % RAW, e * UNIT:(e + 1) * UNIT].rearrange("p (c n) -> p c n", n=P),
                                 w_in_chunks[:, :, c0:c0 + P]).then_inc(raw_in[d % RAW], 16)
            for d in range(D_WO, D_UP):
                wait_raw_free(d)
                c0 = 2 * (d - D_WO)
                sp.dma_start(raw[:, d % RAW, :].rearrange("p (c n) -> p c n", n=D),
                             w_out_chunks[:, c0:c0 + 2, :]).then_inc(raw_in[d % RAW], 16)
            with sp.Fori(0, ND // RAW) as i:
                for s in range(RAW):
                    sp.wait_ge(split_lo, i * RAW + (D_UP + s - RAW + 1))
                    sp.dma_start(raw[:, s, :].rearrange("p (c n) -> p c n", n=2 * P),
                                 w_up_chunks[:, :, ds(i * (RAW * 2 * P) + s * 2 * P, 2 * P)]).then_inc(raw_in[s], 16)
            with sp.Fori(0, ND // RAW) as i:
                for s in range(RAW):
                    sp.wait_ge(split_lo, i * RAW + (D_UP + ND + s - RAW + 1))
                    sp.dma_start(raw[:, s, :].rearrange("p (c n) -> p c n", n=D),
                                 w_down_chunks[:, ds(i * (2 * RAW) + 2 * s, 2), :]).then_inc(raw_in[s], 16)
            for t in range(NT):
                for h in range(2):
                    cols = slice(h * HALF, (h + 1) * HALF)
                    sp.wait_ge(y_ready, 2 * t + h + 1)
                    sp.dma_start(out[0, t * P:(t + 1) * P, cols], y_out[t % 2][:, cols]).then_inc(y_stored[t], 16)
            for t in range(NT):
                sp.wait_ge(y_stored[t], 32)

        @block.gpsimd
        def _(pool):
            steps = [0]
            used = [0]

            def link(ins):
                steps[0] += 1
                ins.then_inc(pool_step, 1)
                pool.wait_ge(pool_step, steps[0])

            def diagonal(tile, base, step):
                link(nc.gpsimd.memset(tile[:], 0.0))
                link(nc.gpsimd.affine_select(out=tile[:], in_=tile[:], compare_op=ALU.not_equal, fill=1.0, base=base,
                                             pattern=[[step, P]], channel_multiplier=1))

            diagonal(ident, 0, -1)
            diagonal(reverse, -(P - 1), 1)
            link(nc.gpsimd.memset(rel_tab[BUCKETS:BUCKETS + 1, :], MASKED))
            link(nc.gpsimd.memset(zero16[:], 0.0))
            link(nc.gpsimd.memset(ones[:], 1.0))
            link(nc.gpsimd.memset(nhalf[:], -0.5))
            pool.sem_inc(pool_const, 1)

            def rsqrt(dst, src, n, scale, eps):
                v = shifted[:, used[0]:used[0] + n]
                used[0] += n
                link(nc.gpsimd.tensor_scalar(v, src, scale, eps, ALU.mult, ALU.add))
                return nc.gpsimd.tensor_tensor(dst, v, nhalf[:, 0:n], ALU.pow)

            for t in range(NT):
                pool.wait_ge(x_squared, t + 1)
                rsqrt(r_x[:, t:t + 1], ss_x[:, t:t + 1], 1, 1.0 / D, EPS).then_inc(rx_ready, 1)

            pool.wait_ge(diag_copied, 1)
            pool.dma_start(rows_dram, diag_row).then_inc(rows_out, 16)
            pool.wait_ge(rows_out, 16)
            pool.dma_start(bias.rearrange("p (h n) -> p h n", n=NEAR),
                           bass.AP(rows_dram.tensor, 0, [[1, P], [SPAN, 8], [1, NEAR]])).then_inc(bias_in, 16)

            pool.wait_ge(wp_hi, 1)
            link(nc.gpsimd.tensor_scalar(wp_raw, wp_raw, WS, None, ALU.mult))
            nc.gpsimd.tensor_tensor(wp[:, NG * P:2 * NG * P], wp_raw, wp[:, 0:NG * P], ALU.subtract).then_inc(wp_lo, 1)

            def add_squares(n):
                total = sq_pool[:, 0:SEQ]
                return nc.gpsimd.tensor_tensor(total, total, sq_pool[:, n * SEQ:(n + 1) * SEQ], ALU.add)

            for n in range(NG):
                g = U_ORDER[n]
                w = WINDOWS[g]
                pool.wait_ge(u_copied, n + 1)
                if n == 0:
                    nc.gpsimd.memset(win_a[:, 0:PAD], 0.0)
                    link(nc.gpsimd.memset(win_b[:, 0:PAD], 0.0))
                    pool.wait_ge(const_in, 16 * 10)
                    pool.wait_ge(pad_ready, 1)
                else:
                    pool.wait_ge(mixed_ready, n)
                src, step = u_pad, 1
                dst, other = (win_a, win_b) if g % 2 == 0 else (win_b, win_a)
                while step < w:
                    link(nc.gpsimd.tensor_tensor(dst[:, PAD:], src[:, PAD:], src[:, PAD - step:PAD + SEQ - step],
                                                 ALU.add))
                    src, dst, other, step = dst, other, dst, 2 * step
                nc.gpsimd.tensor_tensor(src[:, PAD:2 * PAD], src[:, PAD:2 * PAD], edges[:, g * PAD:(g + 1) * PAD],
                                        ALU.mult).then_inc(window_ready, 1)
                if n >= 2:
                    pool.wait_ge(pm_sq, n)
                    link(add_squares(n - 1))
            pool.wait_ge(pm_sq, NG)
            add_squares(NG - 1).then_inc(squares_ready, 1)

            pool.wait_ge(branch_ss, 1)
            rsqrt(r_branches, ss_branches, 2 * NT, WS * WS / POOL_W, WS * WS * EPS).then_inc(branch_r_ready, 1)
            for t in range(NT):
                pool.wait_ge(mix_squared, t + 1)
                rsqrt(r_mix[:, t:t + 1], ss_mix[:, t:t + 1], 1, 1.0 / D, EPS).then_inc(rm_ready, 1)
                pool.wait_ge(x1_squared, t + 1)
                rsqrt(r_x1[:, t:t + 1], ss_x1[:, t:t + 1], 1, 1.0 / D, EPS).then_inc(r1_ready, 1)
            for t in range(NT):
                pool.wait_ge(ff_squared, 2 * t + 1)
                link(nc.gpsimd.tensor_scalar(half_ff[:, t:t + 1], ss_ff[:, 2 * t:2 * t + 1], 1.0 / D, WS * WS * EPS,
                                             ALU.mult, ALU.add))
                pool.wait_ge(ff_squared, 2 * t + 2)
                rsqrt(r_ff[:, t:t + 1], ss_ff[:, 2 * t + 1:2 * t + 2], 1, 1.0 / D,
                      half_ff[:, t:t + 1]).then_inc(rf_ready, 1)

        def pre_gain(c):
            return vecs[:, 5 * NG + c:5 * NG + c + 1]

        def split_dst(d, part):
            if d < D_WO:
                return big[:, 2 * d:2 * d + 2, part, :]
            if d < D_UP:
                return wo[:, 2 * (d - D_WO):2 * (d - D_WO) + 2, part, :]
            if d == D_UP + 2 * ND - 1:
                return wo[:, 0:2, part, :]
            r = 2 * (d % 2)
            return ring[:, r:r + 2, part, :]

        def raw_halves(d):
            return raw[:, d % RAW, :].rearrange("p (s n) -> p s n", s=2)

        def split_hi_op(act, d, i=0):
            act.wait_ge(raw_in[d % RAW], i * 16 + loads_until(d))
            nc.scalar.activation(split_dst(d, 0), raw_halves(d), ACT.Copy, scale=WS).then_inc(split_hi, 1)

        def split_lo_op(dve, d, i=0):
            dve.wait_ge(split_hi, i * RAW + (d + 1))
            nc.vector.scalar_tensor_tensor(out=split_dst(d, 1), in0=raw_halves(d), scalar=WS, in1=split_dst(d, 0),
                                           op0=ALU.mult, op1=ALU.subtract).then_inc(split_lo, 1)

        def wo_raw(p):
            return raw_flat[:, ds(p * (2 * UNIT), 2 * UNIT)].rearrange("p (s n) -> p s n", s=2)

        def wo_dst(p, part):
            return wo_flat[:, ds(p * (4 * UNIT), 4 * UNIT)].rearrange("p (s a n) -> p s a n", s=2, a=2)[:, :, part, :]

        @block.scalar
        def _(act):
            act.dma_start(pre_rows, g_mix_pre.rearrange("a (c n) -> (a c) n", n=P)).then_inc(pre_in, 16)
            act.wait_ge(pool_const, 1)
            nc.scalar.activation(junk0[:, 0:1], ones[:], ACT.Square).then_inc(table_loaded, 1)
            act.wait_ge(table_loaded, 1)
            for t in range(NT):
                act.wait_ge(x_in[t], 16)
                if t >= 1:
                    act.wait_ge(x_squared, t)
                nc.scalar.activation(junk0, x_tok[:, t, :], ACT.Square,
                                     accum_out=ss_x[:, t:t + 1]).then_inc(x_squared, 1)

            def first_split_hi(unit, cols):
                return nc.scalar.activation(big[:, unit, 0, cols], raw_halves(0)[:, unit, cols], ACT.Copy, scale=WS)

            def input_hi(chunks):
                for c in chunks:
                    act.wait_ge(xT_mm, c + 1)
                    nc.scalar.activation(hT[:, 0, c, :], bank[c][:], ACT.Copy, scale=pre_gain(c)).then_inc(hT_hi, 1)

            act.wait_ge(raw_in[0], 16)
            first_split_hi(0, slice(0, HALF)).then_inc(first_hi, 1)
            input_hi(range(0, 4))
            first_split_hi(0, slice(HALF, UNIT)).then_inc(first_hi, 1)
            first_split_hi(1, slice(0, UNIT)).then_inc(split_hi, 1)
            input_hi(range(4, KC))
            for d in range(1, D_WO):
                split_hi_op(act, d)
            act.wait_ge(const_in, 16 * 10)
            nc.scalar.activation(wp[:, 0:NG * P], wp_raw, ACT.Copy,
                                 scale=WS).then_inc(wp_hi, 1)
            for t in range(NT):
                act.wait_ge(v_mm, t + 1)
                nc.scalar.activation(v_hi[:, t, :], bank[t][:], ACT.Copy, scale=1 / WS).then_inc(v_hi_done, 1)

            def qk_parts(p):
                act.wait_ge(qk_proj, 2 * p + 2)
                nc.scalar.activation(kT[:, 0, :], J[0][:], ACT.Copy, scale=1 / WS).then_inc(qk_hi, 1)
                nc.scalar.activation(by_tile(qT[:, 0, :]), q_reversed, ACT.Copy, scale=1 / WS / 8).then_inc(qk_hi, 1)

            def exp_step(p, s):
                n = (s % NT + 1) * P
                act.wait_ge(max_ready, p * STEPS + (s + 1))
                if s >= 2:
                    act.wait_ge(pT_mm, p * STEPS + (s - 1))
                c = s % 4
                nc.scalar.activation(prob[s % 2][:, 0:n], S[s % 2][:, 0:n], ACT.Exp, bias=neg_max[:, c:c + 1],
                                     accum_out=row_sum[:, c:c + 1]).then_inc(exp_done, 1)

            def pool_branch_hi(p, src):
                act.wait_ge(pm_mm, p + 1)
                nc.scalar.activation(sq_pool[:, ds(p * SEQ, SEQ)], src[:], ACT.Square,
                                     scale=vecs[:, ds(p + 3 * NG, 1)]).then_inc(pm_sq, 1)
                nc.scalar.activation(flat[:, ds(p * UNIT + SLOT_YP * 2 * UNIT, SEQ)], src[:], ACT.Copy,
                                     scale=vecs[:, ds(p + 4 * NG, 1)]).then_inc(pm_hi, 1)

            def pair(p, last):
                exp_step(p, 0)
                act.wait_ge(u_mm, p + 1)
                nc.scalar.activation(u_pad[:, PAD:], O[0][:], ACT.Copy, scale=1 / WS).then_inc(u_copied, 1)
                exp_step(p, 1)
                for s in range(STEPS):
                    n = (s % NT + 1) * P
                    act.wait_ge(pT_mm, p * STEPS + (s + 1))
                    if s >= 2:
                        act.wait_ge(pv_mm, p * STEPS + (s - 1))
                    nc.scalar.activation(pT[s % 2][:, 0, 0:n], PT[s % 2][:, 0:n], ACT.Copy).then_inc(pT_hi, 1)
                    if 1 <= s < STEPS - 1:
                        exp_step(p, s + 1)
                    if s == 5:
                        act.wait_ge(pooled, p + 1)
                        nc.scalar.activation(flat[:, ds((p * 3 + SLOT_U) * (2 * UNIT), SEQ)], win_a[:, PAD:],
                                             ACT.Copy).then_inc(mixed_hi, 1)
                if last:
                    pool_branch_hi(p, S[0])
                else:
                    nc.scalar.activation(wo_dst(p, 0), wo_raw(p), ACT.Copy, scale=WS).then_inc(split_hi, 1)
                    act.wait_ge(score_mm, p * STEPS + STEPS)
                    qk_parts(p + 1)
                act.wait_ge(y_normed, p * STEPS + STEPS)
                for t in range(NT):
                    ins = nc.scalar.activation(junk1[:, t * P:(t + 1) * P], y_tok[:, t, :], ACT.Square,
                                               accum_out=ss_attn[:, ds(p * NT + t, 1)])
                ins.then_inc(y_squared, 1)
                act.wait_ge(yT_mm, p + 1)
                y_chunk = flat[:, ds(p * UNIT, SEQ)]
                nc.scalar.activation(y_chunk, PT[0][:], ACT.Copy,
                                     scale=vecs[:, ds(p + 2 * NG, 1)]).then_inc(yT_hi, 1)
                if not last:
                    pool_branch_hi(p, O[1])
                act.wait_ge(y_squared, p + 1)

            qk_parts(0)
            for d in range(D_WO, D_WO + NPAIR - 1):
                act.wait_ge(raw_in[d % RAW], loads_until(d))
            with act.Fori(0, NPAIR - 1) as p:
                pair(p, False)
            pair(NPAIR - 1, True)

            act.wait_ge(mixed_ready, NG)
            for row, gain in ((row_mix_post, g_mix_post), (row_mlp_pre, g_mlp_pre), (row_mlp_post, g_mlp_post)):
                act.dma_start(row, bass.AP(gain.tensor, gain.offset, [[0, P], [1, D]])).then_inc(late_rows_in, 16)
            for d in range(D_UP - 1, D_UP + 2):
                if d == D_UP - 1:
                    act.wait_ge(wp_lo, 1)
                    act.wait_ge(vec_ready, 3)
                    act.wait_ge(rows_out, 16)
                split_hi_op(act, d)

            def pool_share(t):
                for h in range(2):
                    act.wait_ge(outp_mm, 2 * t + h + 1)
                    nc.scalar.activation(mix(t)[:, h * HALF:(h + 1) * HALF], out_bank("pool", t, h)[:], ACT.Copy,
                                         scale=r_pool[:, t:t + 1]).then_inc(outp_scaled, 1)

            def mix_square(t):
                act.wait_ge(mix_ready, 2 * (t + 1))
                if t >= 1:
                    act.wait_ge(x1_squared, t)
                nc.scalar.activation(junk2, mix(t), ACT.Square, accum_out=ss_mix[:, t:t + 1]).then_inc(mix_squared, 1)

            def x1_square(t):
                act.wait_ge(x1_ready, t + 1)
                act.wait_ge(mix_squared, t + 1)
                nc.scalar.activation(junk2, x_tok[:, t, :], ACT.Square,
                                     accum_out=ss_x1[:, t:t + 1]).then_inc(x1_squared, 1)

            def input2_hi(t):
                for h in range(2):
                    act.wait_ge(x1T_mm, 2 * t + h + 1)
                    nc.scalar.activation(hT[:, 0, 4 * h:4 * h + 4, t * P:(t + 1) * P],
                                         J[h][:].rearrange("p (c n) -> p c n", n=P), ACT.Copy).then_inc(h2_hi, 1)

            act.wait_ge(branch_r_ready, 1)
            pool_share(0)
            pool_share(1)
            mix_square(0)
            x1_square(0)
            mix_square(1)
            x1_square(1)
            pool_share(2)
            input2_hi(0)
            input2_hi(1)
            mix_square(2)
            pool_share(3)
            x1_square(2)
            input2_hi(2)
            mix_square(3)
            x1_square(3)
            input2_hi(3)

            with act.Fori(0, ND // RAW) as i:
                for dd in range(RAW):
                    for e in range(2):
                        j = 2 * dd + e
                        act.wait_ge(up_mm, i * (2 * RAW) + (j + 1))
                        if j >= 2:
                            act.wait_ge(sq_done, i * (2 * RAW) + (j - 1))
                        nc.scalar.activation(relu[j % 2], bank[j % 4][:], ACT.Relu, scale=1 / WS).then_inc(relu_done, 1)
                        act.wait_ge(relu_done, i * (2 * RAW) + (j + 1))
                        nc.scalar.activation(flat[:, ds(i * (2 * RAW * UNIT) + j * UNIT, SEQ)], relu[j % 2],
                                             ACT.Square).then_inc(a_hi, 1)
                    split_hi_op(act, D_UP + 2 + dd, i)
                act.wait_ge(sq_done, i * (2 * RAW) + 2 * RAW)
            with act.Fori(0, ND // RAW - 1) as i:
                for dd in range(RAW):
                    act.wait_ge(down_mm, i * RAW + (dd + 1))
                    split_hi_op(act, D_UP + ND + 2 + dd, i)
            act.wait_ge(down_mm, ND - RAW + 1)
            split_hi_op(act, D_UP + 2 * ND - 2)
            split_hi_op(act, D_UP + 2 * ND - 1)
            for t in range(NT):
                for h in range(2):
                    act.wait_ge(ff_done, 2 * t + h + 1)
                    if 2 * t + h:
                        act.wait_ge(ff_squared, 2 * t + h)
                    nc.scalar.activation(junk2[:, 0:HALF], bank[2 * t + h][:], ACT.Square,
                                         accum_out=ss_ff[:, 2 * t + h:2 * t + h + 1]).then_inc(ff_squared, 1)

        @block.vector
        def _(dve):
            dve.sem_inc(yT_lo, 1)
            dve.sem_inc(pm_lo, 1)
            dve.wait_ge(gain_mm, 1)
            nc.vector.tensor_copy(vecs[:, 5 * NG:5 * NG + KC], bank[7][:, 0:KC]).then_inc(gain_ready, 1)
            for t in range(NT):
                dve.wait_ge(rx_ready, t + 1)
                nc.vector.tensor_scalar(xs[t], x_tok[:, t, :], r_x[:, t:t + 1], None, ALU.mult).then_inc(xs_ready, 1)
            dve.wait_ge(gain_ready, 1)

            def input_lo(chunks):
                for c in chunks:
                    dve.wait_ge(hT_hi, c + 1)
                    nc.vector.scalar_tensor_tensor(out=hT[:, 1, c, :], in0=bank[c][:], scalar=pre_gain(c),
                                                   in1=hT[:, 0, c, :], op0=ALU.mult,
                                                   op1=ALU.subtract).then_inc(hT_lo, 1)

            def first_split_lo(unit, cols):
                return nc.vector.scalar_tensor_tensor(out=big[:, unit, 1, cols], in0=raw_halves(0)[:, unit, cols],
                                                      scalar=WS, in1=big[:, unit, 0, cols], op0=ALU.mult,
                                                      op1=ALU.subtract)

            dve.wait_ge(first_hi, 1)
            first_split_lo(0, slice(0, HALF)).then_inc(first_lo, 1)
            input_lo(range(0, 4))
            dve.wait_ge(first_hi, 2)
            first_split_lo(0, slice(HALF, UNIT)).then_inc(first_lo, 1)
            dve.wait_ge(split_hi, 1)
            first_split_lo(1, slice(0, UNIT)).then_inc(split_lo, 1)
            input_lo(range(4, KC))
            split_lo_op(dve, 1)
            split_lo_op(dve, 2)
            dve.wait_ge(diag_mm, 1)
            nc.vector.tensor_copy(diag_row, bank[4][0:8, 0:SPAN]).then_inc(diag_copied, 1)
            dve.wait_ge(vec_mm, 1)
            nc.vector.tensor_copy(vecs[:, 0:3 * NG], bank[5][:, 0:3 * NG]).then_inc(vec_ready, 1)
            dve.wait_ge(vec_ready, 1)
            nc.vector.tensor_scalar(vecs[:, 3 * NG:4 * NG], vecs[:, 0:NG], 1 / WS, None,
                                    ALU.mult).then_inc(vec_ready, 1)
            dve.wait_ge(vec_ready, 2)
            nc.vector.tensor_tensor(vecs[:, 4 * NG:5 * NG], vecs[:, 3 * NG:4 * NG], vecs[:, NG:2 * NG],
                                    ALU.mult).then_inc(vec_ready, 1)
            nc.vector.memset(u_pad[:, 0:PAD], 0.0).then_inc(pad_ready, 1)
            for d in range(3, D_WO):
                split_lo_op(dve, d)
            for t in range(NT):
                dve.wait_ge(v_hi_done, t + 1)
                nc.vector.scalar_tensor_tensor(out=v_lo[:, t, :], in0=bank[t][:], scalar=1 / WS, in1=v_hi[:, t, :],
                                               op0=ALU.mult, op1=ALU.subtract).then_inc(v_lo_done, 1)
            def qk_parts(p):
                dve.wait_ge(qk_hi, 2 * p + 1)
                nc.vector.scalar_tensor_tensor(out=kT[:, 1, :], in0=J[0][:], scalar=1 / WS, in1=kT[:, 0, :],
                                               op0=ALU.mult, op1=ALU.subtract).then_inc(qk_lo, 1)
                dve.wait_ge(qk_hi, 2 * p + 2)
                nc.vector.scalar_tensor_tensor(out=by_tile(qT[:, 1, :]), in0=q_reversed, scalar=1 / WS / 8,
                                               in1=by_tile(qT[:, 0, :]), op0=ALU.mult,
                                               op1=ALU.subtract).then_inc(qk_lo, 1)

            def max_step(p, s):
                i, h, b = s % NT, s // NT, s % 2
                n = (i + 1) * P
                near = min(NEAR, n)
                dve.wait_ge(score_mm, p * STEPS + (s + 1))
                nc.vector.tensor_tensor(S[b][:, n - near:n], S[b][:, n - near:n],
                                        bias[:, ds(p * (2 * NEAR) + (h * NEAR + NEAR - near), near)],
                                        ALU.add).then_inc(biased, 1)
                dve.wait_ge(biased, p * STEPS + (s + 1))
                c = s % 4
                nc.vector.tensor_reduce(neg_max[:, c:c + 1], S[b][:, 0:n], AX, ALU.max,
                                        negate=True).then_inc(max_ready, 1)

            def norm_step(p, s):
                i, h = s % NT, s // NT
                c = s % 4
                dve.wait_ge(pv_mm, p * STEPS + (s + 1))
                dve.wait_ge(inv_ready, p * STEPS + (s + 1))
                nc.vector.tensor_scalar(y_tok[:, i, h * HD:(h + 1) * HD], O[s % 2][:, 0:HD], row_inv[:, c:c + 1],
                                        None, ALU.mult).then_inc(y_normed, 1)

            def pool_branch_lo(p, src):
                dve.wait_ge(pm_sq, p + 1)
                dve.wait_ge(pm_hi, p + 1)
                place = p * UNIT + SLOT_YP * 2 * UNIT
                nc.vector.scalar_tensor_tensor(out=flat[:, ds(place + SEQ, SEQ)], in0=src[:],
                                               scalar=vecs[:, ds(p + 4 * NG, 1)], in1=flat[:, ds(place, SEQ)],
                                               op0=ALU.mult, op1=ALU.subtract).then_inc(pm_lo, 1)

            def pair(p, last):
                for s in range(STEPS):
                    if s + 1 < STEPS:
                        max_step(p, s + 1)
                    n = (s % NT + 1) * P
                    c = s % 4
                    dve.wait_ge(exp_done, p * STEPS + (s + 1))
                    nc.vector.reciprocal(row_inv[:, c:c + 1], row_sum[:, c:c + 1]).then_inc(inv_ready, 1)
                    dve.wait_ge(pT_hi, p * STEPS + (s + 1))
                    nc.vector.tensor_tensor(pT[s % 2][:, 1, 0:n], PT[s % 2][:, 0:n], pT[s % 2][:, 0, 0:n],
                                            ALU.subtract).then_inc(pT_lo, 1)
                    if s >= 1:
                        norm_step(p, s - 1)
                    if s == 4:
                        dve.wait_ge(window_ready, p + 1)
                        nc.vector.scalar_tensor_tensor(out=win_a[:, PAD:], in0=win_a[:, PAD:],
                                                       scalar=edges[:, ds(p + NG * PAD, 1)], in1=u_pad[:, PAD:],
                                                       op0=ALU.mult, op1=ALU.subtract).then_inc(pooled, 1)
                    if s == 6:
                        dve.wait_ge(mixed_hi, p + 1)
                        place = (p * 3 + SLOT_U) * (2 * UNIT)
                        nc.vector.tensor_tensor(flat[:, ds(place + SEQ, SEQ)], win_a[:, PAD:],
                                                flat[:, ds(place, SEQ)], ALU.subtract).then_inc(mixed_ready, 1)
                if not last:
                    qk_parts(p + 1)
                norm_step(p, STEPS - 1)
                if not last:
                    dve.wait_ge(split_hi, p + (D_WO + 1))
                    nc.vector.scalar_tensor_tensor(out=wo_dst(p, 1), in0=wo_raw(p), scalar=WS, in1=wo_dst(p, 0),
                                                   op0=ALU.mult, op1=ALU.subtract).then_inc(split_lo, 1)
                else:
                    pool_branch_lo(p, S[0])
                dve.wait_ge(yT_hi, p + 1)
                dve.wait_ge(y_squared, p + 1)
                nc.vector.scalar_tensor_tensor(out=flat[:, ds(p * UNIT + SEQ, SEQ)], in0=PT[0][:],
                                               scalar=vecs[:, ds(p + 2 * NG, 1)], in1=flat[:, ds(p * UNIT, SEQ)],
                                               op0=ALU.mult, op1=ALU.subtract).then_inc(yT_lo, 1)
                if not last:
                    max_step(p + 1, 0)
                    pool_branch_lo(p, O[1])

            qk_parts(0)
            dve.wait_ge(bias_in, 16)
            max_step(0, 0)
            with dve.Fori(0, NPAIR - 1) as p:
                pair(p, False)
            pair(NPAIR - 1, True)

            dve.wait_ge(y_squared, NPAIR)
            nc.vector.tensor_reduce(ss_attn_sum, ss_attn.rearrange("p (c t) -> p t c", c=NPAIR), AX,
                                    ALU.add).then_inc(attn_ss, 1)
            split_lo_op(dve, D_UP - 1)
            dve.wait_ge(branch_ss_mm, 1)
            nc.vector.tensor_copy(ss_branches, S[1][:, 0:2 * NT]).then_inc(branch_ss, 1)
            split_lo_op(dve, D_UP)
            split_lo_op(dve, D_UP + 1)
            dve.wait_ge(branch_r_ready, 1)
            dve.wait_ge(late_rows_in, 16 * 3)

            def add_shares(t):
                for h in range(2):
                    dve.wait_ge(outa_mm, 2 * t + h + 1)
                    dve.wait_ge(outp_scaled, 2 * t + h + 1)
                    m = mix(t)[:, h * HALF:(h + 1) * HALF]
                    nc.vector.scalar_tensor_tensor(out=m, in0=out_bank("attn", t, h)[:], scalar=r_attn[:, t:t + 1],
                                                   in1=m, op0=ALU.mult, op1=ALU.add).then_inc(mix_ready, 1)

            def residual(t):
                dve.wait_ge(rm_ready, t + 1)
                nc.vector.scalar_tensor_tensor(out=mix(t), in0=mix(t), scalar=r_mix[:, t:t + 1], in1=row_mix_post,
                                               op0=ALU.mult, op1=ALU.mult).then_inc(mix_scaled, 1)
                dve.wait_ge(mix_scaled, t + 1)
                nc.vector.tensor_tensor(x_tok[:, t, :], x_tok[:, t, :], mix(t), ALU.add).then_inc(x1_ready, 1)

            def norm_x1(t):
                dve.wait_ge(r1_ready, t + 1)
                if t >= 2:
                    dve.wait_ge(x1T_mm, 2 * (t - 1))
                nc.vector.scalar_tensor_tensor(out=xs2[t % 2], in0=x_tok[:, t, :], scalar=r_x1[:, t:t + 1],
                                               in1=row_mlp_pre, op0=ALU.mult, op1=ALU.mult).then_inc(xs2_ready, 1)

            def input2_lo(t):
                for h in range(2):
                    dve.wait_ge(h2_hi, 2 * t + h + 1)
                    nc.vector.tensor_tensor(hT[:, 1, 4 * h:4 * h + 4, t * P:(t + 1) * P],
                                            J[h][:].rearrange("p (c n) -> p c n", n=P),
                                            hT[:, 0, 4 * h:4 * h + 4, t * P:(t + 1) * P],
                                            ALU.subtract).then_inc(h2_lo, 1)

            add_shares(0)
            residual(0)
            add_shares(1)
            norm_x1(0)
            residual(1)
            input2_lo(0)
            norm_x1(1)
            add_shares(2)
            input2_lo(1)
            residual(2)
            norm_x1(2)
            add_shares(3)
            input2_lo(2)
            residual(3)
            norm_x1(3)
            input2_lo(3)

            with dve.Fori(0, ND // RAW) as i:
                for dd in range(RAW):
                    for e in range(2):
                        j = 2 * dd + e
                        dve.wait_ge(relu_done, i * (2 * RAW) + (j + 1))
                        if j >= 2:
                            dve.wait_ge(a_lo, i * (2 * RAW) + (j - 1))
                        nc.vector.tensor_tensor(squared[j % 2], relu[j % 2], relu[j % 2], ALU.mult).then_inc(sq_done, 1)
                        dve.wait_ge(sq_done, i * (2 * RAW) + (j + 1))
                        dve.wait_ge(a_hi, i * (2 * RAW) + (j + 1))
                        nc.vector.tensor_tensor(flat[:, ds(i * (2 * RAW * UNIT) + (j * UNIT + SEQ), SEQ)],
                                                squared[j % 2],
                                                flat[:, ds(i * (2 * RAW * UNIT) + j * UNIT, SEQ)],
                                                ALU.subtract).then_inc(a_lo, 1)
                    split_lo_op(dve, D_UP + 2 + dd, i)
                dve.wait_ge(a_lo, i * (2 * RAW) + 2 * RAW)
            with dve.Fori(0, ND // RAW - 1) as i:
                for dd in range(RAW):
                    split_lo_op(dve, D_UP + ND + 2 + dd, i)
            for dd in range(2):
                split_lo_op(dve, D_UP + 2 * ND - 2 + dd)

            for t in range(NT):
                halves = [slice(h * HALF, (h + 1) * HALF) for h in range(2)]
                if t >= 2:
                    dve.wait_ge(y_stored[t - 2], 32)
                for h in range(2):
                    dve.wait_ge(ff_squared, 2 * t + h + 1)
                    nc.vector.tensor_tensor(y_out[t % 2][:, halves[h]], bank[2 * t + h][:], row_mlp_post[:, halves[h]],
                                            ALU.mult).then_inc(ff_scaled, 1)
                dve.wait_ge(ff_scaled, 2 * t + 2)
                dve.wait_ge(rf_ready, t + 1)
                for h in range(2):
                    y = y_out[t % 2][:, halves[h]]
                    nc.vector.scalar_tensor_tensor(out=y, in0=y, scalar=r_ff[:, t:t + 1], in1=x_tok[:, t, halves[h]],
                                                   op0=ALU.mult, op1=ALU.add).then_inc(y_ready, 1)

        @block.tensor
        def _(pe):
            def passes(dst, w_hi, w_lo, m_hi, m_lo, first, final):
                nc.tensor.matmul(dst, w_hi, m_hi, start=first, stop=False)
                nc.tensor.matmul(dst, w_hi, m_lo, start=False, stop=False)
                return nc.tensor.matmul(dst, w_lo, m_hi, start=False, stop=final)

            pe.wait_ge(pool_const, 1)
            pe.wait_ge(pre_in, 16)
            nc.tensor.transpose(bank[7][:, 0:KC], pre_rows, ident[0:KC, 0:KC]).then_inc(gain_mm, 1)
            for t in range(NT):
                pe.wait_ge(xs_ready, t + 1)
                for c in range(KC):
                    ins = nc.tensor.transpose(bank[c][:, t * P:(t + 1) * P], xs[t][:, c * P:(c + 1) * P], ident[:])
                    if t == NT - 1:
                        ins.then_inc(xT_mm, 1)
            for c in range(KC):
                pe.wait_ge(hT_lo, max(c + 1, NT))
                if c < 2:
                    pe.wait_ge(first_lo, c + 1)
                elif c == 2 or c == 4:
                    pe.wait_ge(split_lo, c // 2)
                w = big[:, SLOT_V + c // 2, :, (c % 2) * HALF:(c % 2) * HALF + HALF]
                for t in range(NT):
                    ins = passes(bank[t][:], hT[:, 0, c, t * P:(t + 1) * P], hT[:, 1, c, t * P:(t + 1) * P],
                                 w[:, 0, :], w[:, 1, :], c == 0, c == KC - 1)
                    if c == KC - 1:
                        ins.then_inc(v_mm, 1)
                if c == 4:
                    pe.wait_ge(hT_lo, 6)
                    pe.wait_ge(const_in, 16 * 10)
                    nc.tensor.matmul(bank[4][0:8, 0:SPAN], rel_tab, onehot, start=True, stop=True).then_inc(diag_mm, 1)
                    nc.tensor.transpose(bank[5][:, 0:3 * NG], vec_rows, ident[0:3 * NG, 0:3 * NG]).then_inc(vec_mm, 1)

            def project(dst, slot, chunks):
                for c in chunks:
                    ins = passes(dst, flat[:, ds(slot * (2 * UNIT) + c * P, P)],
                                 flat[:, ds(slot * (2 * UNIT) + (UNIT + c * P), P)],
                                 hT[:, 0, c, :], hT[:, 1, c, :], c == 0, c == KC - 1)
                return ins

            def scores(p, s):
                i, h, b = s % NT, s // NT, s % 2
                n = (i + 1) * P
                if s >= 2:
                    pe.wait_ge(exp_done, p * STEPS + (s - 1))
                rows = slice(h * HD, (h + 1) * HD)
                passes(S[b][:, 0:n], qT[rows, 0, i * P:(i + 1) * P], qT[rows, 1, i * P:(i + 1) * P],
                       kT[rows, 0, 0:n], kT[rows, 1, 0:n], True, True).then_inc(score_mm, 1)

            def transpose_probs(p, s):
                pe.wait_ge(exp_done, p * STEPS + (s + 1))
                if s == 0:
                    pe.wait_ge(yT_lo, p + 1)
                for j in range(s % NT + 1):
                    ins = nc.tensor.transpose(PT[s % 2][:, j * P:(j + 1) * P], prob[s % 2][:, j * P:(j + 1) * P],
                                              ident[:])
                ins.then_inc(pT_mm, 1)

            def outputs(p, s):
                i, h, b = s % NT, s // NT, s % 2
                pe.wait_ge(pT_lo, p * STEPS + (s + 1))
                if s >= 2:
                    pe.wait_ge(y_normed, p * STEPS + (s - 1))
                for j in range(i + 1):
                    cols = ds(p * P + h * HD, HD)
                    ins = passes(O[b][:, 0:HD], pT[b][:, 0, j * P:(j + 1) * P], pT[b][:, 1, j * P:(j + 1) * P],
                                 v_hi[:, j, cols], v_lo[:, j, cols], j == 0, j == i)
                ins.then_inc(pv_mm, 1)

            def fill(p, s):
                chunks = range(2 * (s % 4), 2 * (s % 4) + 2)
                if s < 4:
                    ins = project(J[1][:], p * 3 + (SLOT_Q + 3), chunks)
                else:
                    ins = project(J[0][:], p * 3 + (SLOT_K + 3), chunks)
                if s % 4 == 3:
                    ins.then_inc(qk_proj, 1)

            def pool_product(p, dst):
                pe.wait_ge(mixed_ready, p + 1)
                place = (p * 3 + SLOT_U) * (2 * UNIT)
                passes(dst[:], wp[:, ds(p * P, P)], wp[:, ds(p * P + NG * P, P)], flat[:, ds(place, SEQ)],
                       flat[:, ds(place + SEQ, SEQ)], True, True).then_inc(pm_mm, 1)

            def out_chunks(i, chunks):
                br, t, h = out_groups[i]
                for n in chunks:
                    y, w_chunk = (y_half(SLOT_YP, n), U_ORDER[n]) if br == "pool" else (y_half(SLOT_YA, n), NG + n)
                    w = wo[:, w_chunk, :, h * HALF:(h + 1) * HALF]
                    ins = passes(out_bank(br, t, h)[:], y[:, 0, t * P:(t + 1) * P], y[:, 1, t * P:(t + 1) * P],
                                 w[:, 0, :], w[:, 1, :], n == 0, n == NG - 1)
                if n == NG - 1:
                    ins.then_inc(outp_mm if br == "pool" else outa_mm, 1)

            def pair(p, last):
                pe.wait_ge(qk_lo, p * 2 + 2)
                scores(p, 0)
                scores(p, 1)
                project(O[0][:], p * 3 + SLOT_U, range(4, 8)).then_inc(u_mm, 1)
                transpose_probs(p, 0)
                for s in range(STEPS):
                    if s + 2 < STEPS:
                        scores(p, s + 2)
                    if s + 1 < STEPS:
                        transpose_probs(p, s + 1)
                    if not last:
                        fill(p, s)
                    elif s < 6:
                        if s == 4:
                            pe.wait_ge(pm_lo, NG)
                        out_chunks(s % 2, [s // 2])
                    elif s == STEPS - 1:
                        pool_product(p, S[0])
                    if s == 1:
                        pe.wait_ge(pm_lo, p + 1)
                    if s == 0:
                        pe.wait_ge(u_copied, p + 1)
                    outputs(p, s)
                if not last:
                    pe.wait_ge(y_normed, p * STEPS + (STEPS - 1))
                    project(O[0][:], p * 3 + (SLOT_U + 3), range(0, 4))
                pe.wait_ge(y_normed, p * STEPS + STEPS)
                for t in range(NT):
                    ins = nc.tensor.transpose(PT[0][:, t * P:(t + 1) * P], y_tok[:, t, :], reverse[:])
                ins.then_inc(yT_mm, 1)
                if not last:
                    pool_product(p, O[1])

            pe.wait_ge(split_lo, 3)
            pe.wait_ge(hT_lo, KC)
            project(J[1][:], SLOT_Q, range(KC)).then_inc(qk_proj, 1)
            project(J[0][:], SLOT_K, range(KC)).then_inc(qk_proj, 1)
            pe.wait_ge(split_lo, D_WO)
            project(O[0][:], SLOT_U, range(0, 4))
            pe.wait_ge(v_lo_done, NT)
            pe.wait_ge(wp_lo, 1)
            with pe.Fori(0, NPAIR - 1) as p:
                pair(p, False)
            pair(NPAIR - 1, True)

            def transpose_x1(t):
                pe.wait_ge(xs2_ready, t + 1)
                for h in range(2):
                    if t >= 1:
                        pe.wait_ge(h2_lo, 2 * (t - 1) + h + 1)
                    for c in range(4):
                        ins = nc.tensor.transpose(J[h][:, c * P:(c + 1) * P],
                                                  xs2[t % 2][:, (4 * h + c) * P:(4 * h + c + 1) * P], ident[:])
                    ins.then_inc(x1T_mm, 1)

            for i in range(2, 4):
                out_chunks(i, range(NG - 1))
            pe.wait_ge(pm_lo, NG + 1)
            for i in range(4):
                out_chunks(i, [NG - 1])
                if i == 1:
                    pe.wait_ge(squares_ready, 1)
                    for t in range(NT):
                        nc.tensor.matmul(S[1][:, t:t + 1], sq_pool[:, t * P:(t + 1) * P], ones[:], start=True,
                                         stop=True)
                    pe.wait_ge(attn_ss, 1)
                    nc.tensor.matmul(S[1][:, NT:2 * NT], reverse[:], ss_attn_sum, start=True,
                                     stop=True).then_inc(branch_ss_mm, 1)
            pe.wait_ge(yT_lo, NPAIR + 1)
            for i in range(4, len(out_groups)):
                br, t, h = out_groups[i]
                if (br, t, h) == ("attn", 0, 0):
                    pe.wait_ge(split_lo, D_UP)
                if (br, t, h) == ("attn", 1, 1):
                    pe.wait_ge(branch_ss, 1)
                if (br, t, h) == ("attn", 2, 0):
                    pe.wait_ge(outp_scaled, 2)
                    transpose_x1(0)
                if (br, t, h) == ("pool", 3, 0):
                    transpose_x1(1)
                if i >= 8:
                    before, t0, h0 = out_groups[i - 6]
                    pe.wait_ge(outp_scaled if before == "pool" else mix_ready, 2 * t0 + h0 + 1)
                out_chunks(i, range(NG))
            transpose_x1(2)

            def up(j, e, r, cols=slice(0, SEQ)):
                for c in range(KC):
                    w = slice((c % 4) * 2 * P + e * P, (c % 4) * 2 * P + (e + 1) * P)
                    ins = passes(bank[j][:, cols], ring[:, r + c // 4, 0, w], ring[:, r + c // 4, 1, w],
                                 hT[:, 0, c, cols], hT[:, 1, c, cols], c == 0, c == KC - 1)
                return ins

            pe.wait_ge(split_lo, D_UP + 1)
            pe.wait_ge(h2_lo, 2 * (NT - 2))
            pe.wait_ge(outp_scaled, 2 * NT)
            up(0, 0, 0, slice(0, SEQ - 2 * P))
            pe.wait_ge(h2_lo, 2 * (NT - 1))
            up(0, 0, 0, slice(SEQ - 2 * P, SEQ - P))
            up(1, 1, 0, slice(0, SEQ - P))
            pe.wait_ge(split_lo, D_UP + 2)
            up(2, 0, 2, slice(0, P))
            transpose_x1(NT - 1)
            up(2, 0, 2, slice(P, SEQ - P))
            pe.wait_ge(h2_lo, 2 * NT)
            for j in range(3):
                up(j, j % 2, j // 2 * 2, slice(SEQ - P, SEQ)).then_inc(up_mm, 1)
            up(3, 1, 2).then_inc(up_mm, 1)
            with pe.Fori(1, ND // 2) as i:
                for dd in range(2):
                    pe.wait_ge(split_lo, i * 2 + (D_UP + dd + 1))
                    for e in range(2):
                        up(2 * dd + e, e, 2 * dd).then_inc(up_mm, 1)

            pe.wait_ge(relu_done, NF)
            for b in range(2 * NT):
                nc.tensor.matmul(bank[b][:, 0:1], zero16[:], zero16[:, 0:1], start=True, stop=False,
                                 skip_group_check=True)

            def down(j, w, tiles, halves=(0, 1)):
                for t in tiles:
                    for h in halves:
                        for part_a, part_w in ((0, 0), (0, 1), (1, 0)):
                            ins = nc.tensor.matmul(bank[2 * t + h][:],
                                                   flat[:, ds(j * UNIT + (part_a * SEQ + t * P), P)],
                                                   w[:, part_w, h * HALF:(h + 1) * HALF], start=False,
                                                   stop=False, skip_group_check=True)
                return ins

            with pe.Fori(0, ND // RAW - 1) as i:
                for dd in range(RAW):
                    pe.wait_ge(split_lo, i * RAW + (D_UP + ND + dd + 1))
                    pe.wait_ge(a_lo, i * (2 * RAW) + (2 * dd + 2))
                    for e in range(2):
                        ins = down(i * (2 * RAW) + (2 * dd + e), ring[:, 2 * (dd % 2) + e], range(NT))
                    ins.then_inc(down_mm, 1)
            pe.wait_ge(a_lo, NF)
            for dd in range(2):
                pe.wait_ge(split_lo, D_UP + 2 * ND - RAW + dd + 1)
                for e in range(2):
                    ins = down(NF - 2 * RAW + 2 * dd + e, ring[:, 2 * dd + e], range(NT))
                ins.then_inc(down_mm, 1)
            pe.wait_ge(split_lo, D_UP + 2 * ND)
            for t in range(NT):
                for h in range(2):
                    for e in range(4):
                        ins = down(NF - 4 + e, ring[:, e] if e < 2 else wo[:, e - 2], [t], [h])
                    ins.then_inc(ff_done, 1)


_INS = ['x', 'w_in', 'w_pool', 'pool_scale', 'rel_bias', 'g_mix_pre', 'g_pool_out', 'g_attn_out', 'w_out',
        'g_mix_post', 'g_mlp_pre', 'w_up', 'w_down', 'g_mlp_post']


def _shape_constants():
    import math as _math
    import numpy as _np
    dist = NEAR - 1 - _np.arange(SPAN)
    exact = BUCKETS // 2
    far = _np.log(_np.maximum(dist, exact).astype(_np.float32) / _np.float32(exact)) / _np.float32(_math.log(8.0))
    bucket = _np.where(dist < exact, _np.maximum(dist, 0),
                       _np.minimum(exact + (far * _np.float32(BUCKETS - exact)).astype(_np.int32), BUCKETS - 1))
    rows = _np.zeros((BUCKETS + 1, SPAN), _np.float32)
    rows[bucket, _np.arange(SPAN)] = 1.0
    rows[BUCKETS - 1] -= 1.0
    rows[BUCKETS] = dist < 0
    edges = [w / min(t + 1, w) for w in WINDOWS for t in range(PAD)] + [1 / WINDOWS[g] for g in U_ORDER]
    return rows, _np.array([edges], _np.float32)


def kernel(**inputs):
    import numpy as _np
    import concourse.bacc as _bacc
    from concourse import mybir as _mybir
    from concourse.bass_utils import run_bass_kernel_spmd as _run

    nc = _bacc.Bacc("TRN2", target_bir_lowering=False, num_devices=1)
    rows, edges = _shape_constants()
    arrays, args = {}, []
    for name, a in [(n, inputs[n]) for n in _INS] + [("bucket_rows", rows), ("edge_table", edges)]:
        a = _np.ascontiguousarray(a)
        arrays[f"in_{name}_dram"] = a
        args.append(nc.dram_tensor(f"in_{name}_dram", a.shape, _mybir.dt.from_np(a.dtype), kind="ExternalInput").ap())
    args.append(nc.dram_tensor("out_0_dram", (1, SEQ, D), _mybir.dt.float32, kind="ExternalOutput").ap())
    hybrid_layer(nc, *args)
    r = _run(nc, [arrays], core_ids=[0])
    return r.results[0]["out_0_dram"]
```
